# Optimizing a Trainium2 kernel written in Bass

```python
import jax, jax.numpy as jnp
from jax import lax
import numpy as np

D_MODEL = 1024
BATCH = 1
SEQ = 512
DEPTH = 2

CHUNK = 64
N_MEM = 256
EPS = 1e-6
NEG = -1e30
LB_FLOOR = 1e-30
A_HEADS = 4
A_KEY = 128
A_VAL = 128
A_QK = A_HEADS * A_KEY
A_OV = A_HEADS * A_VAL
B_CH = 512
B_KW = 31
EVEN_IN = 2 * A_QK + 2 * A_OV + 2 * B_CH
EVEN_SPLITS = (A_QK, 2 * A_QK, 2 * A_QK + A_OV, 2 * A_QK + 2 * A_OV, 2 * A_QK + 2 * A_OV + B_CH)
EVEN_MIX = A_OV + B_CH
C_QH = 16
C_KVH = 4
C_HD = 64
C_GROUP = C_QH // C_KVH
WINDOW = 128
WIN_CHUNKS = WINDOW // CHUNK
C_QKV = (C_QH + 2 * C_KVH) * C_HD
C_MIX = C_QH * C_HD
X_HEADS = 4
X_HD = D_MODEL // X_HEADS
X_WIDTH = X_HEADS * X_HD
FFN_HIDDEN = -(-8 * D_MODEL // (3 * 256)) * 256
N_EVEN = (DEPTH + 1) // 2
N_ODD = DEPTH // 2

kernel_name = 'hybrid_hgrn2_conformer_swa_sink_trunk'

def rmsnorm(x, g):
    x32 = x.astype(jnp.float32)
    y = x32 * lax.rsqrt(jnp.mean(x32 * x32, axis=-1, keepdims=True) + EPS)
    return (y * g.astype(jnp.float32)).astype(x.dtype)

def layernorm(x, g, b):
    x32 = x.astype(jnp.float32)
    mu = jnp.mean(x32, axis=-1, keepdims=True)
    xc = x32 - mu
    y = xc * lax.rsqrt(jnp.mean(xc * xc, axis=-1, keepdims=True) + EPS)
    return (y * g.astype(jnp.float32) + b.astype(jnp.float32)).astype(x.dtype)

def alibi_slopes(n):
    return jnp.asarray(2.0 ** (-8.0 * np.arange(1, n + 1) / n), dtype=jnp.float32)

def hgrn2_mixer(q, fz, iv, g, lb, out_norm):
    bsz, seq, _ = q.shape
    n_chunks = seq // CHUNK
    f32 = jnp.float32
    lb = jnp.clip(lb.astype(f32), LB_FLOOR, 1.0 - 1e-6)
    log_f = jnp.logaddexp(jnp.log(lb), jnp.log1p(-lb) + jax.nn.log_sigmoid(fz.astype(f32)))
    k = -jnp.expm1(log_f)

    def to_chunks(t):
        return t.astype(f32).reshape(bsz, n_chunks, CHUNK, A_HEADS, -1).transpose(1, 0, 3, 2, 4)

    qc = to_chunks(q) * (A_KEY ** -0.5)
    kc = to_chunks(k)
    vc = to_chunks(iv)
    bc = jnp.cumsum(to_chunks(log_f), axis=3)
    causal = jnp.tril(jnp.ones((CHUNK, CHUNK), dtype=bool))[:, :, None]

    def step(state, inp):
        q_c, k_c, v_c, b_c = inp
        o_inter = jnp.einsum('bhtk,bhkv->bhtv', q_c * jnp.exp(b_c), state)
        diff = b_c[:, :, :, None, :] - b_c[:, :, None, :, :]
        decay = jnp.exp(jnp.where(causal, diff, NEG))
        scores = jnp.sum(q_c[:, :, :, None, :] * decay * k_c[:, :, None, :, :], axis=-1)
        o = o_inter + jnp.einsum('bhts,bhsv->bhtv', scores, v_c)
        b_last = b_c[:, :, -1:, :]
        state = jnp.exp(b_last[:, :, 0, :, None]) * state + jnp.einsum(
            'bhsk,bhsv->bhkv', k_c * jnp.exp(b_last - b_c), v_c)
        return state, o

    state0 = jnp.zeros((bsz, A_HEADS, A_KEY, A_VAL), f32)
    _, o = lax.scan(step, state0, (qc, kc, vc, bc))
    o = o.transpose(1, 0, 3, 2, 4).reshape(bsz, seq, A_HEADS, A_VAL)
    gate = jax.nn.silu(g.astype(f32)).reshape(bsz, seq, A_HEADS, A_VAL)
    o = rmsnorm(o, out_norm) * gate
    return o.reshape(bsz, seq, A_OV).astype(q.dtype)

def conformer_conv(a, gate, conv_w, conv_b, ln_g, ln_b):
    u = a * jax.nn.sigmoid(gate)
    y = lax.conv_general_dilated(
        u, conv_w[:, None, :].astype(u.dtype), window_strides=(1,),
        padding=[(B_KW - 1, 0)], dimension_numbers=('NWC', 'WIO', 'NWC'),
        feature_group_count=B_CH) + conv_b
    return jax.nn.silu(layernorm(y, ln_g, ln_b))

def swa_sink_attention(h, w_qkv, b_qkv, sinks, w_o, b_o):
    bsz, seq, _ = h.shape
    n_chunks = seq // CHUNK
    qkv = h @ w_qkv + b_qkv
    q, k, v = jnp.split(qkv, [C_QH * C_HD, (C_QH + C_KVH) * C_HD], axis=-1)
    q = q.reshape(bsz, n_chunks, CHUNK, C_KVH, C_GROUP, C_HD)
    k = k.reshape(bsz, n_chunks, CHUNK, C_KVH, C_HD)
    v = v.reshape(bsz, n_chunks, CHUNK, C_KVH, C_HD)
    pad = ((0, 0), (WIN_CHUNKS - 1, 0), (0, 0), (0, 0), (0, 0))
    kp = jnp.pad(k, pad)
    vp = jnp.pad(v, pad)
    kb = jnp.concatenate([kp[:, j:j + n_chunks] for j in range(WIN_CHUNKS)], axis=2)
    vb = jnp.concatenate([vp[:, j:j + n_chunks] for j in range(WIN_CHUNKS)], axis=2)
    s = jnp.einsum('bnqkgd,bnskd->bnkgqs', q, kb).astype(jnp.float32) * (C_HD ** -0.5)
    qi = jnp.arange(CHUNK)[:, None]
    sj = jnp.arange(WIN_CHUNKS * CHUNK)[None, :]
    dist = jnp.abs((WIN_CHUNKS - 1) * CHUNK + qi - sj).astype(jnp.float32)
    slopes = alibi_slopes(C_QH).reshape(C_KVH, C_GROUP)
    s = s - slopes[:, :, None, None] * dist
    cidx = jnp.arange(n_chunks)[:, None]
    valid = sj >= (WIN_CHUNKS - 1 - cidx) * CHUNK
    s = jnp.where(valid[None, :, None, None, None, :], s, NEG)
    sink = sinks.astype(jnp.float32).reshape(C_KVH, C_GROUP)[None, None, :, :, None, None]
    m = jnp.maximum(jnp.max(s, axis=-1, keepdims=True), sink)
    p = jnp.exp(s - m)
    p = p / (jnp.sum(p, axis=-1, keepdims=True) + jnp.exp(sink - m))
    o = jnp.einsum('bnkgqs,bnskd->bnqkgd', p.astype(vb.dtype), vb).reshape(bsz, seq, C_MIX)
    return o @ w_o + b_o

def memory_cross_attention(h, memn, w_q, w_kv, w_o):
    bsz, seq, _ = h.shape
    q = (h @ w_q).reshape(bsz, seq, X_HEADS, X_HD)
    k, v = jnp.split(memn @ w_kv, 2, axis=-1)
    k = k.reshape(bsz, -1, X_HEADS, X_HD)
    v = v.reshape(bsz, -1, X_HEADS, X_HD)
    s = jnp.einsum('bthd,bmhd->bhtm', q, k).astype(jnp.float32) * (X_HD ** -0.5)
    p = jax.nn.softmax(s, axis=-1).astype(v.dtype)
    o = jnp.einsum('bhtm,bmhd->bthd', p, v).reshape(bsz, seq, X_WIDTH)
    return o @ w_o

def swiglu_ffn(h, w_in, w_out):
    gt, up = jnp.split(h @ w_in, 2, axis=-1)
    return (jax.nn.silu(gt) * up) @ w_out

def setup_inputs(seed: int = 0) -> dict:
    key = jax.random.key(seed)
    ks = jax.random.split(key, 25)
    f32 = jnp.float32
    d = D_MODEL

    def nrm(k, shape, scale):
        return jax.random.normal(k, shape, f32) * scale

    def gain(k, shape):
        return 1.0 + 0.02 * jax.random.normal(k, shape, f32)

    return {
        'x': nrm(ks[0], (BATCH, SEQ, d), 1.0),
        'mem': nrm(ks[1], (BATCH, N_MEM, d), 1.0),
        'norm_mix': gain(ks[2], (DEPTH, d)),
        'norm_xattn': gain(ks[3], (DEPTH, d)),
        'norm_ffn': gain(ks[4], (DEPTH, d)),
        'norm_mem': gain(ks[5], (d,)),
        'norm_final': gain(ks[6], (d,)),
        'even_w_in': nrm(ks[7], (N_EVEN, d, EVEN_IN), d ** -0.5),
        'even_w_out': nrm(ks[8], (N_EVEN, EVEN_MIX, d), EVEN_MIX ** -0.5),
        'hgrn_lb_logits': nrm(ks[9], (N_EVEN, A_QK), 0.5),
        'hgrn_out_norm': gain(ks[10], (N_EVEN, A_HEADS, A_VAL)),
        'conv_w': nrm(ks[11], (N_EVEN, B_KW, B_CH), B_KW ** -0.5),
        'conv_b': nrm(ks[12], (N_EVEN, B_CH), 0.02),
        'conv_ln_g': gain(ks[13], (N_EVEN, B_CH)),
        'conv_ln_b': nrm(ks[14], (N_EVEN, B_CH), 0.02),
        'swa_w_qkv': nrm(ks[15], (N_ODD, d, C_QKV), d ** -0.5),
        'swa_b_qkv': nrm(ks[16], (N_ODD, C_QKV), 0.02),
        'swa_sinks': nrm(ks[17], (N_ODD, C_QH), 1.0),
        'swa_w_o': nrm(ks[18], (N_ODD, C_MIX, d), C_MIX ** -0.5),
        'swa_b_o': nrm(ks[19], (N_ODD, d), 0.02),
        'xattn_w_q': nrm(ks[20], (DEPTH, d, X_WIDTH), d ** -0.5),
        'xattn_w_kv': nrm(ks[21], (DEPTH, d, 2 * X_WIDTH), d ** -0.5),
        'xattn_w_o': nrm(ks[22], (DEPTH, X_WIDTH, d), X_WIDTH ** -0.5),
        'ffn_w_in': nrm(ks[23], (DEPTH, d, 2 * FFN_HIDDEN), d ** -0.5),
        'ffn_w_out': nrm(ks[24], (DEPTH, FFN_HIDDEN, d), FFN_HIDDEN ** -0.5),
    }

def reference(x, mem, norm_mix, norm_xattn, norm_ffn, norm_mem, norm_final,
              even_w_in, even_w_out, hgrn_lb_logits, hgrn_out_norm,
              conv_w, conv_b, conv_ln_g, conv_ln_b,
              swa_w_qkv, swa_b_qkv, swa_sinks, swa_w_o, swa_b_o,
              xattn_w_q, xattn_w_kv, xattn_w_o, ffn_w_in, ffn_w_out):
    p_lb = jax.nn.softmax(hgrn_lb_logits.astype(jnp.float32), axis=0)
    lb_all = jnp.cumsum(p_lb, axis=0) - p_lb[0:1]
    memn = rmsnorm(mem, norm_mem)
    for l in range(DEPTH):
        h = rmsnorm(x, norm_mix[l])
        if l % 2 == 0:
            e = l // 2
            z = h @ even_w_in[e]
            q, fz, iv, g, ga, gg = jnp.split(z, EVEN_SPLITS, axis=-1)
            o_a = hgrn2_mixer(q, fz, iv, g, lb_all[e], hgrn_out_norm[e])
            o_b = conformer_conv(ga, gg, conv_w[e], conv_b[e], conv_ln_g[e], conv_ln_b[e])
            mix = jnp.concatenate([o_a, o_b], axis=-1) @ even_w_out[e]
        else:
            o = l // 2
            mix = swa_sink_attention(h, swa_w_qkv[o], swa_b_qkv[o], swa_sinks[o], swa_w_o[o], swa_b_o[o])
        x = x + mix
        x = x + memory_cross_attention(rmsnorm(x, norm_xattn[l]), memn,
                                       xattn_w_q[l], xattn_w_kv[l], xattn_w_o[l])
        x = x + swiglu_ffn(rmsnorm(x, norm_ffn[l]), ffn_w_in[l], ffn_w_out[l])
    return rmsnorm(x, norm_final)


_drawn_inputs = setup_inputs


def setup_inputs(seed=0):
    import zlib

    import numpy as np

    out = dict(_drawn_inputs(seed))
    spreads = {}
    factors = {'norm_xattn': 8.0,
     'norm_ffn': 3.068,
     'norm_mem': 8.0,
     'norm_final': 2.738,
     'hgrn_out_norm': 6.162,
     'conv_b': 2.933,
     'conv_ln_g': 5.193,
     'conv_ln_b': 6.03,
     'swa_b_qkv': 3.743,
     'swa_sinks': 7.592,
     'swa_b_o': 3.52}
    for name, (base, spread) in spreads.items():
        noise = np.random.default_rng([zlib.crc32(name.encode()), seed]).standard_normal(out[name].shape)
        drawn = base * np.exp(spread * noise) if base else spread * noise
        out[name] = __import__('jax').numpy.asarray(drawn.astype(out[name].dtype))
    for name, factor in factors.items():
        out[name] = (out[name] * factor).astype(out[name].dtype)
    return out
```

```python
from contextlib import ExitStack

import numpy as np

import concourse.bass as bass
from concourse import mybir

F32 = mybir.dt.float32
F32R = mybir.dt.float32r
U32 = mybir.dt.uint32
ALU = mybir.AluOpType
ACT = mybir.ActivationFunctionType
AX_X = mybir.AxisListType.X

P = 128
D = 1024
SEQ = 512
N_MEM = 256
KT = D // P
TT = SEQ // P
MT = N_MEM // P
EPS = 1e-6
LB_FLOOR = 1e-30
A_HEADS = 4
B_CH = 512
CT = B_CH // P
B_KW = 31
PAD = B_KW - 1
DVE_TAPS = 24
CHUNK = 64
C_QH = 16
C_HD = 64
WIN = 192
X_HEADS = 4
X_HD = 256
HIDDEN = 2816
FF_GROUPS = (8, 8, 6)
LEVELS = (64, 32, 16, 8, 4, 2, 1)
LN2_50 = 50.0 * float(np.log(2.0))

V_MIX, V_XATTN, V_FFN, V_MEM, V_FINAL = 0, 16, 32, 48, 56
V_LB, V_ONORM, V_CONVB, V_LNG, V_LNB = 64, 68, 72, 76, 80
V_BQ, V_BKV, V_BO = 84, 92, 96
V_ROWS = 104


class Stage:

    def __init__(self, name, quads, kt, width, dmas):
        self.name, self.quads, self.kt, self.width, self.dmas = name, quads, kt, width, dmas
        self.first = 0
        self.landed = 0
        self.next = None


def plan_stages():
    stages = [Stage("E", 6, 8, SEQ, 1), Stage("EO", 2, 8, SEQ, 1)]
    for layer in range(2):
        if layer:
            stages += [Stage("QKV", 3, 8, SEQ, 2), Stage("SO", 2, 8, SEQ, 4)]
        stages += [Stage(f"KV{layer}", 4, 8, N_MEM, 1), Stage(f"XQ{layer}", 2, 8, SEQ, 1),
                   Stage(f"XO{layer}", 2, 8, SEQ, 1)]
        for n, tiles in enumerate(FF_GROUPS):
            stages += [Stage(f"FI{layer}{n}", tiles // 2, 8, SEQ, 1), Stage(f"FO{layer}{n}", 2, tiles, SEQ, 1)]
    first = landed = 0
    for s, after in zip(stages, stages[1:] + [None]):
        s.first, s.landed, s.next = first, landed, after
        first += 4 * s.quads
        landed += 16 * s.dmas * s.quads
    return {s.name: s for s in stages}, first


def trunk_kernel(nc, a, consts, out):
    stages, _ = plan_stages()
    ctx = ExitStack()
    with ctx:
        def sb(name, shape, dt=F32):
            return ctx.enter_context(nc.sbuf_tensor(name, [P, *shape], dt))

        def sem(name):
            return ctx.enter_context(nc.semaphore(name))

        x = sb("x", [KT, SEQ])
        a_hi, a_lo = sb("a_hi", [KT, SEQ], F32R), sb("a_lo", [KT, SEQ], F32R)
        b_at = nc.sbuf_base
        b_hi, b_lo = sb("b_hi", [KT, SEQ], F32R), sb("b_lo", [KT, SEQ], F32R)
        b_end = nc.sbuf_base
        w_raw = sb("w_raw", [4, KT, P])
        w_hi, w_lo = sb("w_hi", [4, KT, P], F32R), sb("w_lo", [4, KT, P], F32R)
        m_hi, m_lo = sb("m_hi", [KT, N_MEM], F32R), sb("m_lo", [KT, N_MEM], F32R)
        row_scale = sb("row_scale", [SEQ])
        sumsq = sb("sumsq", [SEQ])
        sq = sb("sq", [2, SEQ])
        diag = sb("diag", [TT, P])
        ident = sb("ident", [P])
        ones = sb("ones", [P])
        vec = sb("vec", [V_ROWS])
        minus_half = sb("minus_half", [16])
        stat = sb("stat", [160])
        used = [0]

        def small(n):
            used[0] += n
            return stat[:, used[0] - n:used[0]]

        ms, rstd, cvar_m, cvar_r = small(TT), small(TT), small(TT), small(TT)
        o_m, o_r = small(TT), small(TT)
        mem_ss, mem_m, mem_rs = small(MT), small(MT), small(MT)
        xs_negmax, xs_sum, xs_rec = small(TT), small(TT), small(TT)
        ss_negmax, ss_sum, ss_rec = (small(4).rearrange("p (a b) -> p a b", a=2) for _ in range(3))
        lb_d, lb_e, lb_r, lb_v, lb_rest, lb_half = (small(A_HEADS) for _ in range(6))
        ln_rest, ln_scaled, ln_lb = (small(A_HEADS) for _ in range(3))
        edge = small(TT)
        onorm_half, lng_half, lnb_half = small(A_HEADS), small(CT), small(CT)
        sink8 = small(C_QH)
        s_dist, s_slope = sb("s_dist", [2, WIN]), sb("s_slope", [C_QH])
        arena_floats = (nc.sbuf_bytes_remaining - 64) // 4
        arena = sb("arena", [arena_floats])
        early = nc.alloc_sbuf_tensor_at("early", [P, 4, 4, SEQ], F32, offset=b_at)
        assert b_end - b_at >= 4 * 4 * SEQ * 4

        class Carve:
            def __init__(self, at=0):
                self.at = at

            def __call__(self, *shape):
                n = int(np.prod(shape))
                assert self.at + n <= arena_floats, (self.at + n, arena_floats)
                v = arena[:, self.at:self.at + n]
                self.at += n
                if len(shape) == 2:
                    v = v.rearrange("p (a b) -> p a b", a=shape[0])
                elif len(shape) == 3:
                    v = v.rearrange("p (a b c) -> p a b c", a=shape[0], b=shape[1])
                return v

        carve = Carve()
        conv_y = carve(CT, SEQ)
        hg_k = carve(A_HEADS, SEQ)
        scan_mask = carve(SEQ)
        lev_mask = carve(len(LEVELS), P)
        conv_w = carve(P)
        heads_at = carve.at
        u_pad = carve(CT, PAD + SEQ)
        conv_b2, conv_p, conv_pt = carve(SEQ), carve(SEQ), carve(SEQ)
        e_gate, e_tanh, e_half = carve(SEQ), carve(SEQ), carve(SEQ)
        carve = Carve(heads_at)
        pre_1, pre_2 = carve(A_HEADS, SEQ), carve(A_HEADS, SEQ)
        ln_t = carve(CT, SEQ)
        carve = Carve(heads_at)
        hg_e, hg_qk = carve(4, SEQ), carve(2, SEQ)
        hg_scores, hg_qe = carve(TT, P), carve(SEQ)
        hg_kd_tok, hg_v_tok, hg_state = carve(3, P), carve(TT, P), carve(3, P)
        hg_sq, hg_on, hg_out = carve(TT, P), carve(TT, P), carve(SEQ)
        x_tok = Carve(heads_at)(TT, D)
        mem_tok, mem_sq = Carve(CT * SEQ)(MT, D), Carve(arena_floats - D)(D)
        vec_rows = Carve(0)(2 * P)
        hg_q, hg_b, hg_v, hg_g = (early[:, n] for n in range(4))
        carve = Carve()
        x_k, x_v = carve(KT, N_MEM), carve(MT, D)
        late_at = carve.at
        v_feat = carve(2, N_MEM)
        carve = Carve(late_at)
        x_q, x_p, x_pt = carve(2, 2, SEQ), carve(TT, N_MEM), carve(MT, SEQ)
        carve = Carve(late_at)
        f_gate, f_tanh, f_silu, f_act = carve(2, SEQ), carve(2, SEQ), carve(2, SEQ), carve(2, SEQ)
        carve = Carve()
        s_k, s_vf = carve(2, 64 + SEQ), carve(2, 64 + SEQ)
        s_v = carve(2, 5, P)
        s_q = carve(2, SEQ)
        s_s, s_e = carve(2, 2, WIN + 1), carve(2, 2, WIN + 1)
        s_p, s_pt = carve(2, 2, WIN), carve(2, SEQ)
        o_tok = Carve()(TT, D)

        gemm_ps = [ctx.enter_context(nc.psum_tensor(f"gemm_ps{n}", [P, SEQ], F32)) for n in range(4)]
        aux_ps = [ctx.enter_context(nc.psum_tensor(f"aux_ps{n}", [P, SEQ], F32)) for n in range(4)]

        consts_in, params_in, x_in, mem_in, stored = (
            sem(n) for n in ("consts_in", "params_in", "x_in", "mem_in", "stored"))
        w_landed = [sem(f"w_landed{n}") for n in range(4)]
        w_hi_ready, w_lo_ready, block_done, block_taken = (
            sem(n) for n in ("w_hi_ready", "w_lo_ready", "block_done", "block_taken"))
        act_hi_ready, act_lo_ready = sem("act_hi_ready"), sem("act_lo_ready")
        sq_ready, sumsq_added, sumsq_clear, norm_ps, norm_ms, norm_rstd, norm_diag, norm_wide, norm_ready = (
            sem(n) for n in ("sq_ready", "sumsq_added", "sumsq_clear", "norm_ps", "norm_ms", "norm_rstd",
                             "norm_diag", "norm_wide", "norm_ready"))
        fills_ready, pad_ready, vec_turned, vec_ready, xt_done, xt_taken = (
            sem(n) for n in ("fills_ready", "pad_ready", "vec_turned", "vec_ready", "xt_done", "xt_taken"))
        vector_step, pool_step = sem("vector_step"), sem("pool_step")
        gate_tanh, gated, pool_conv, conv_merged = (
            sem(n) for n in ("gate_tanh", "gated", "pool_conv", "conv_merged"))
        mean_wide, centred, cvar_sq, cvar_ps, cvar_ms, cvar_rstd, cvar_diag, cvar_wide, ln_out, ln_tanh, ln_act = (
            sem(n) for n in ("mean_wide", "centred", "cvar_sq", "cvar_ps", "cvar_ms", "cvar_rstd", "cvar_diag",
                             "cvar_wide", "ln_out", "ln_tanh", "ln_act"))
        lb_diff, lb_exp, lb_ready, lb_logs, neg_abs, key_tanh, log1p_a, log_pair, log1p_b, gates_ready = (
            sem(n) for n in ("lb_diff", "lb_exp", "lb_ready", "lb_logs", "neg_abs", "key_tanh", "log1p_a",
                             "log_pair", "log1p_b", "gates_ready"))
        scalar_step = sem("scalar_step")
        kd_ready, qe_exp, qe_ready, edge_ready, vt_ps, vt_ready, kdt_ps, kdt_ready = (
            sem(n) for n in ("kd_ready", "qe_exp", "qe_ready", "edge_ready", "vt_ps",
                             "vt_ready", "kdt_ps", "kdt_ready"))
        e_arg, e_exp, lev_ready, lev_ps, lev_taken, st_ps, st_ready = (
            sem(n) for n in ("e_arg", "e_exp", "lev_ready", "lev_ps", "lev_taken", "st_ps", "st_ready"))
        o_ps, o_sq, o_ms, o_rstd, on_ready, ont_ps, og_ready = (
            sem(n) for n in ("o_ps", "o_sq", "o_ms", "o_rstd", "on_ready", "ont_ps", "og_ready"))
        mem_sq_ready, mem_ms, mem_rstd, mem_scaled, memt_ps, mem_hi, mem_lo, vf_turned, vf_taken = (
            sem(n) for n in ("mem_sq_ready", "mem_ms", "mem_rstd", "mem_scaled", "memt_ps", "mem_hi", "mem_lo",
                             "vf_turned", "vf_taken"))
        xs_ps, xs_max, xs_exp, xs_norm, xpt_ps, xpt_ready, xo_ps = (
            sem(n) for n in ("xs_ps", "xs_max", "xs_exp", "xs_norm", "xpt_ps", "xpt_ready", "xo_ps"))
        f_tanh_ready, f_silu_ready = sem("f_tanh_ready"), sem("f_silu_ready")
        sv_pad, sv_ps, sv_ready, ss_ps, ss_ready, ss_max, ss_exp, ss_norm, spt_ps, spt_ready, so_ps = (
            sem(n) for n in ("sv_pad", "sv_ps", "sv_ready", "ss_ps", "ss_ready", "ss_max", "ss_exp", "ss_norm",
                             "spt_ps", "spt_ready", "so_ps"))
        sq_biased = sem("sq_biased")
        fin_scaled, fin_ps, fin_even, fin_odd = (sem(n) for n in ("fin_scaled", "fin_ps", "fin_even", "fin_odd"))

        block = ctx.enter_context(nc.Block())

        def wait(eng, s, value):
            if not (isinstance(value, int) and value <= 0):
                eng.wait_ge(s, value)

        TILES = {}
        count = 0
        for name, n in [("x0", 8), ("mix0", 8), ("x1", 8), ("att0", 8), ("x2", 8), ("h00", 8), ("h01", 8), ("h02", 6),
                        ("x3", 8), ("mix1", 8), ("x4", 8), ("att1", 8), ("x5", 8), ("h10", 8), ("h11", 8), ("h12", 6)]:
            TILES[name] = count
            count += n
        G_COLS = [V_MIX, V_XATTN, V_FFN, V_MIX + 8, V_XATTN + 8, V_FFN + 8, V_FINAL]

        def run_quads(eng, stage, body, whole=False):
            n = stage.quads
            peel = whole or stage.next is None or stage.next.dmas != stage.dmas
            if n - peel > 0:
                with eng.Fori(0, n - peel) as i:
                    body(i, False)
            if peel:
                body(n - 1, True)

        def landed(stage, i, ahead):
            if ahead and isinstance(i, int) and i == stage.quads - 1:
                return None if stage.next is None else stage.next.landed + 16 * stage.next.dmas
            return (i + 1 + ahead) * (16 * stage.dmas) + stage.landed

        def split_hi(act, stage, i, j):
            g = i * 4 + (stage.first + j + 3)
            slot = (j + 3) % 4
            value = landed(stage, i, 0 if j == 0 else 1)
            if value is None:
                return
            act.wait_ge(w_landed[slot], value)
            wait(act, block_done, g - 3)
            nc.scalar.activation(w_hi[:, slot], w_raw[:, slot], ACT.Copy).then_inc(w_hi_ready, 1)

        def split_lo(dve, stage, i, j):
            g = i * 4 + (stage.first + j + 3)
            slot = (j + 3) % 4
            if landed(stage, i, 0 if j == 0 else 1) is None:
                return
            dve.wait_ge(w_hi_ready, g + 1)
            nc.vector.tensor_tensor(w_lo[:, slot], w_raw[:, slot], w_hi[:, slot].bitcast(F32),
                                    ALU.subtract).then_inc(w_lo_ready, 1)

        def gemm(pe, stage, i, j, hi, lo, tiles, order=None, parts=(0, 1), banks=4):
            g = i * 4 + (stage.first + j)
            order = order or list(range(stage.kt))
            width = stage.width
            start, stop = len(order) * parts[0] // parts[1], len(order) * (parts[0] + 1) // parts[1]
            if parts[1] == 1:
                start, stop = 0, len(order)
            if start == 0:
                pe.wait_ge(w_lo_ready, g + 1)
                wait(pe, block_taken, g + 1 - banks)
            for n in range(start, stop):
                k = order[n]
                if j == 0 and tiles is not None:
                    pe.wait_ge(act_lo_ready, tiles + n + 1)
                first, last = n == 0, n == len(order) - 1
                o = gemm_ps[j % banks][:, 0:width]
                nc.tensor.matmul(o, w_hi[:, j, k], hi[:, k, 0:width], start=first, stop=False)
                nc.tensor.matmul(o, w_hi[:, j, k], lo[:, k, 0:width], start=False, stop=False)
                mm = nc.tensor.matmul(o, w_lo[:, j, k], hi[:, k, 0:width], start=False, stop=last)
            if stop == len(order):
                mm.then_inc(block_done, 1)

        A, B = (a_hi, a_lo), (b_hi, b_lo)

        def column(first, n):
            return vec[:, :].rearrange("p (v o) -> p v o", o=1)[:, n + first]

        def by_chunk(ap):
            return ap.rearrange("p (c q) -> p c q", q=P)

        def rows(w, at):
            w = w.rearrange("(r p) -> r p", p=P)
            return vec_rows[at:at + w.shape[0], 0:P], w

        param_rows = [rows(a[name].rearrange("l d -> (l d)"), at) for name, at in [
            ("norm_mix", V_MIX), ("norm_xattn", V_XATTN), ("norm_ffn", V_FFN), ("hgrn_lb_logits", V_LB),
            ("conv_b", V_CONVB), ("conv_ln_g", V_LNG), ("conv_ln_b", V_LNB), ("swa_b_o", V_BO)]]
        param_rows += [rows(a["norm_mem"], V_MEM), rows(a["norm_final"], V_FINAL),
                       rows(a["hgrn_out_norm"].rearrange("l h d -> (l h d)"), V_ONORM),
                       rows(a["swa_b_qkv"][0, C_QH * C_HD:], V_BKV)]
        bq = a["swa_b_qkv"][0, 0:C_QH * C_HD].rearrange("(a b j d) -> a b j d", a=2, b=2, j=4)
        for i in range(2):
            for b in range(2):
                param_rows.append((vec_rows[V_BQ + 4 * i:V_BQ + 4 * i + 4, 64 * b:64 * b + 64], bq[i, b]))
        param_rows.append((vec_rows[0:B_KW * CT, P:2 * P], a["conv_w"][0].rearrange("k (c p) -> (k c) p", p=P)))

        @block.sync
        def _(sp):
            sp.dma_start(x_tok, a["x"][0].rearrange("(t p) d -> p t d", p=P)).then_inc(x_in, 16)

            def cols(w):
                return w.rearrange("(k p) (b n) -> b p k n", p=P, n=P)

            def load(stage, source, block_of):
                kt = stage.kt

                def quad(i, j):
                    g = i * 4 + (stage.first + j)
                    wait(sp, w_lo_ready, g - 3)
                    sp.dma_start(w_raw[:, j, 0:kt], source[block_of(i, j)]).then_inc(w_landed[j], 16)

                return quad

            def run(stage, quad, lo=0):
                hi = stage.quads
                if hi - lo > 1:
                    with sp.Fori(lo, hi) as i:
                        for j in range(4):
                            quad(i, j)
                elif hi > lo:
                    for j in range(4):
                        quad(lo, j)

            e = cols(a["even_w_in"][0])
            st = stages["E"]
            gg, ga = 2560 // P, 2048 // P
            quad = load(st, e, lambda i, j: i * 2 + ((ga if j % 2 else gg) + j // 2))
            for i in range(2):
                for j in range(4):
                    quad(i, j)
                if i == 0:
                    sp.dma_start(mem_tok, a["mem"][0].rearrange("(m p) d -> p m d", p=P)).then_inc(mem_in, 16)
            run(st, load(st, e, lambda i, j: i * 4 + (j - 8)), 2)

            def plain(name, w):
                run(stages[name], load(stages[name], cols(w), lambda i, j: i * 4 + j))

            def ffn(layer):
                w_in, w_out = a["ffn_w_in"][layer], a["ffn_w_out"][layer]
                at = 0
                for n, tiles in enumerate(FF_GROUPS):
                    st = stages[f"FI{layer}{n}"]
                    run(st, load(st, cols(w_in), lambda i, j, at=at: i * 2 + (at + j // 2 + (HIDDEN // P) * (j % 2))))
                    plain(f"FO{layer}{n}", w_out[at * P:(at + tiles) * P])
                    at += tiles

            plain("EO", a["even_w_out"][0])
            for layer in range(2):
                if layer:
                    wq = a["swa_w_qkv"][0].rearrange("(k p) (h d) -> h p k d", p=P, d=C_HD)
                    st = stages["QKV"]
                    for j in range(4):
                        sp.wait_ge(w_lo_ready, st.first + j - 3)
                        for b in range(2):
                            sp.dma_start(w_raw[:, j, :, b * 64:b * 64 + 64], wq[C_QH + 2 * j + b]).then_inc(w_landed[j], 16)
                    for i in range(2):
                        for j in range(4):
                            sp.wait_ge(w_lo_ready, st.first + 4 + 4 * i + j - 3)
                            for b in range(2):
                                sp.dma_start(w_raw[:, j, :, b * 64:b * 64 + 64],
                                             wq[8 * i + j + 4 * b]).then_inc(w_landed[j], 16)
                    wo = a["swa_w_o"][0].rearrange("(a b j d) (c n) -> c a b d j n", a=2, b=2, j=4, n=P)
                    st = stages["SO"]
                    with sp.Fori(0, 2) as i:
                        for j in range(4):
                            sp.wait_ge(w_lo_ready, i * 4 + (st.first + j - 3))
                            for half_ in range(2):
                                for b in range(2):
                                    sp.dma_start(w_raw[b * 64:b * 64 + 64, j, 4 * half_:4 * half_ + 4, :],
                                                 wo[i * 4 + j, half_, b]).then_inc(w_landed[j], 16)
                plain(f"KV{layer}", a["xattn_w_kv"][layer])
                plain(f"XQ{layer}", a["xattn_w_q"][layer])
                plain(f"XO{layer}", a["xattn_w_o"][layer])
                ffn(layer)
            o_rows = out[0].rearrange("(t p) d -> p t d", p=P)
            for t in range(TT):
                sp.wait_ge(fin_even, t + 1)
                sp.wait_ge(fin_odd, t + 1)
                sp.dma_start(o_rows[:, t], o_tok[:, t]).then_inc(stored, 16)
            sp.wait_ge(stored, 16 * TT)

        @block.tensor
        def _(pe):
            def transpose(o, i_, size=P):
                return nc.tensor.transpose(o, i_, ident[0:size, 0:size])

            pe.wait_ge(consts_in, 16 * 5)
            pe.wait_ge(params_in, 16 * len(param_rows))
            transpose(aux_ps[0][:, 0:V_ROWS], vec_rows[0:V_ROWS, 0:P], V_ROWS)
            transpose(aux_ps[0][:, P:P + B_KW * CT], vec_rows[0:B_KW * CT, P:2 * P],
                      B_KW * CT).then_inc(vec_turned, 1)
            pe.wait_ge(x_in, 16)
            for n in range(KT):
                wait(pe, xt_taken, n - 3)
                for t in range(TT):
                    mm = transpose(gemm_ps[n % 4][:, t * P:(t + 1) * P], x_tok[:, t, n * P:(n + 1) * P])
                mm.then_inc(xt_done, 1)

            def norm_sums(n):
                pe.wait_ge(sumsq_added, 8 * (n + 1))
                for t in range(TT):
                    mm = nc.tensor.matmul(aux_ps[3][:, t:t + 1], sumsq[:, t * P:(t + 1) * P], ones[:, 0:1],
                                          start=True, stop=True)
                mm.then_inc(norm_ps, 1)

            def norm_spread(n):
                pe.wait_ge(norm_diag, n + 1)
                nc.tensor.matmul(aux_ps[2][:, :], ones[:, :], diag[:, :, :], start=True, stop=True).then_inc(norm_wide, 1)

            def first_quad(stage, inp, tiles, n):
                gemm(pe, stage, 0, 0, *inp, tiles)
                norm_sums(n)
                gemm(pe, stage, 0, 1, *inp, tiles)
                norm_spread(n)
                gemm(pe, stage, 0, 2, *inp, tiles)
                gemm(pe, stage, 0, 3, *inp, tiles)

            def plain(stage, inp, tiles, lo=0, order=None):
                if stage.quads > lo:
                    with pe.Fori(lo, stage.quads) as i:
                        for j in range(4):
                            gemm(pe, stage, i, j, *inp, tiles, order)

            pe.wait_ge(xt_taken, 8)
            first_quad(stages["E"], A, TILES["x0"], 0)
            for j in range(4):
                gemm(pe, stages["E"], 1, j, *A, None)
            pe.wait_ge(mem_scaled, MT)
            for n in range(KT):
                wait(pe, mem_lo, n - 1)
                for m in range(MT):
                    mm = transpose(aux_ps[n % 2][:, m * P:(m + 1) * P], mem_tok[:, m, n * P:(n + 1) * P])
                mm.then_inc(memt_ps, 1)
            plain(stages["E"], A, None, 2)

            for c in range(CT):
                pe.wait_ge(conv_merged, c + 1)
                mm = nc.tensor.matmul(aux_ps[2][:, :], ones[:, :], conv_y[:, c], start=c == 0, stop=c == CT - 1)
            mm.then_inc(mean_wide, 1)
            pe.wait_ge(cvar_sq, CT)
            for t in range(TT):
                for c in range(CT):
                    mm = nc.tensor.matmul(aux_ps[3][:, t:t + 1], ln_t[:, c, t * P:(t + 1) * P], ones[:, 0:1],
                                          start=c == 0, stop=c == CT - 1)
            mm.then_inc(cvar_ps, 1)
            pe.wait_ge(cvar_diag, 1)
            nc.tensor.matmul(aux_ps[3][:, :], ones[:, :], diag[:, :, :], start=True, stop=True).then_inc(cvar_wide, 1)

            def turn_outputs(h):
                pe.wait_ge(on_ready, h + 1)
                for c in range(TT):
                    mm = transpose(aux_ps[2][:, c * P:(c + 1) * P], hg_on[:, c])
                mm.then_inc(ont_ps, 1)

            for h in range(A_HEADS):
                wait(pe, vt_ready, h)
                for c in range(TT):
                    mm = transpose(gemm_ps[1][:, c * P:(c + 1) * P], hg_v[:, h, c * P:(c + 1) * P])
                mm.then_inc(vt_ps, 1)
                pe.wait_ge(gates_ready, 1)
                wait(pe, lev_taken, h * 8)
                for c in range(TT):
                    s = slice(c * P, (c + 1) * P)
                    mm = nc.tensor.matmul(aux_ps[0][:, s], hg_k[:, h, s], hg_q[:, h, s], start=True, stop=True)
                mm.then_inc(lev_ps, 1)
                pe.wait_ge(kd_ready, h + 1)
                wait(pe, kdt_ready, h)
                for c in range(3):
                    mm = transpose(gemm_ps[0][:, c * P:(c + 1) * P], hg_e[:, 0, c * P:(c + 1) * P])
                mm.then_inc(kdt_ps, 1)

                def level(n):
                    pe.wait_ge(lev_ready, h * 7 + (n + 1))
                    wait(pe, lev_taken, h * 8 + n)
                    for c in range(TT):
                        s = slice(c * P, (c + 1) * P)
                        qk = hg_qk[:, n % 2, s]
                        mm = nc.tensor.matmul(aux_ps[(n + 1) % 2][:, s], qk, qk, start=True, stop=True)
                    mm.then_inc(lev_ps, 1)

                level(0)
                pe.wait_ge(kdt_ready, h + 1)
                pe.wait_ge(vt_ready, h + 1)
                for c in range(3):
                    mm = nc.tensor.matmul(gemm_ps[2][:, c * P:(c + 1) * P], hg_kd_tok[:, c], hg_v_tok[:, c],
                                          start=True, stop=True)
                mm.then_inc(st_ps, 1)
                level(1)
                if h:
                    turn_outputs(h - 1)
                for n in range(2, len(LEVELS)):
                    level(n)
                pe.wait_ge(lev_taken, h * 8 + 8)
                pe.wait_ge(st_ready, h * 3 + 3)
                pe.wait_ge(qe_ready, h + 1)
                for c in range(TT):
                    s = slice(c * P, (c + 1) * P)
                    mm = nc.tensor.matmul(gemm_ps[3][:, s], hg_scores[:, c], hg_v_tok[:, c], start=True, stop=c == 0)
                    if c:
                        mm = nc.tensor.matmul(gemm_ps[3][:, s], hg_qe[:, s], hg_state[:, c - 1], start=False, stop=True)
                mm.then_inc(o_ps, 1)
            turn_outputs(A_HEADS - 1)

            def cross_attention(layer, tiles_in):
                st = stages[f"XQ{layer}"]
                inp = B
                done = 4 * layer

                def scores(h):
                    pe.wait_ge(block_taken, st.first + 2 * h + 2)
                    pe.wait_ge(xs_exp, done + h)
                    pe.wait_ge(vf_taken, 8 * layer + 8)
                    for t in range(TT):
                        for d in range(2):
                            mm = nc.tensor.matmul(aux_ps[t // 2][:, (t % 2) * N_MEM:(t % 2 + 1) * N_MEM],
                                                  x_q[:, h % 2, d, t * P:(t + 1) * P], x_k[:, 2 * h + d],
                                                  start=d == 0, stop=d == 1)
                    mm.then_inc(xs_ps, 1)

                def turn(h):
                    pe.wait_ge(xs_norm, done + h + 1)
                    pe.wait_ge(act_lo_ready, TILES[f"att{layer}"] + 2 * h)
                    for m in range(MT):
                        for t in range(TT):
                            mm = transpose(aux_ps[2 + m][:, t * P:(t + 1) * P], x_p[:, t, m * P:(m + 1) * P])
                    mm.then_inc(xpt_ps, 1)

                def output(h):
                    pe.wait_ge(xpt_ready, done + h + 1)
                    for d in range(2):
                        for m in range(MT):
                            col = h * X_HD + d * P
                            mm = nc.tensor.matmul(aux_ps[2 + d][:, :], x_v[:, m, col:col + P], x_pt[:, m],
                                                  start=m == 0, stop=m == MT - 1)
                        mm.then_inc(xo_ps, 1)

                for h in range(X_HEADS + 2):
                    if h < X_HEADS:
                        gemm(pe, st, h // 2, 2 * (h % 2), *inp, tiles_in if h == 0 else None)
                    if h >= 2:
                        output(h - 2)
                    if 1 <= h <= X_HEADS:
                        scores(h - 1)
                    if h < X_HEADS:
                        gemm(pe, st, h // 2, 2 * (h % 2) + 1, *inp, None)
                    if 1 <= h <= X_HEADS:
                        turn(h - 1)

            def memory_products(layer, n, tiles_in):
                st = stages[f"KV{layer}"]
                mem = (m_hi, m_lo)
                if layer == 0:
                    pe.wait_ge(mem_lo, KT)
                for at in range(8):
                    if at == 1:
                        norm_sums(n)
                    if at == 5:
                        norm_spread(n)
                    gemm(pe, st, at // 4, at % 4, *mem, None)

                def turn(i, j):
                    at = i * 4 + (8 * layer + j - 8)
                    pe.wait_ge(block_taken, i * 4 + (st.first + j + 1))
                    wait(pe, vf_taken, at - 1)
                    for m in range(MT):
                        mm = transpose(aux_ps[j % 2][:, m * P:(m + 1) * P], v_feat[:, j % 2, m * P:(m + 1) * P])
                    mm.then_inc(vf_turned, 1)

                for i in range(2, 4):
                    for j in range(4):
                        gemm(pe, st, i, j, *mem, None)
                        if j:
                            turn(i, j - 1)
                    turn(i, 3)

            def ffn(layer, tiles_in, n):
                for grp in range(3):
                    st, so = stages[f"FI{layer}{grp}"], stages[f"FO{layer}{grp}"]
                    if grp == 0:
                        first_quad(st, B, tiles_in, n)
                        plain(st, B, None, 1)
                    else:
                        plain(st, B, None)
                    plain(so, A, TILES[f"h{layer}{grp}"])

            def window_attention():
                st = stages["QKV"]
                first_quad(st, B, TILES["x3"], 3)
                pe.wait_ge(sv_pad, 2)
                for n in range(2):
                    for m in range(5):
                        rows = 64 if m == 4 else P
                        q = n * 5 + m
                        wait(pe, sv_ready, q - 1)
                        mm = transpose(aux_ps[q % 2][0:rows, 0:P], s_vf[:, n, m * P:m * P + rows])
                        mm.then_inc(sv_ps, 1)

                def scores(w):
                    j, t = w // TT, w % TT
                    pe.wait_ge(sq_biased, j + 1)
                    wait(pe, ss_ready, w - 1)
                    if w < 2:
                        pe.wait_ge(sv_ready, 10)
                    for b in range(2):
                        r = slice(64 * b, 64 * b + 64)
                        mm = nc.tensor.matmul(aux_ps[2 * (w % 2) + b][:, 0:WIN],
                                              s_q[r, j % 2, t * P:(t + 1) * P],
                                              s_k[r, j // 4, t * P:t * P + WIN], start=True, stop=True)
                    mm.then_inc(ss_ps, 1)

                def turn(w):
                    pe.wait_ge(ss_norm, w + 1)
                    wait(pe, spt_ready, w)
                    for b in range(2):
                        transpose(gemm_ps[2][:, 2 * b * P:(2 * b + 1) * P], s_p[:, w % 2, b, 0:P])
                        mm = transpose(gemm_ps[2][0:64, (2 * b + 1) * P:(2 * b + 2) * P], s_p[:, w % 2, b, P:WIN])
                    mm.then_inc(spt_ps, 1)

                def output(w):
                    j, t = w // TT, w % TT
                    pe.wait_ge(spt_ready, w + 1)
                    if t == 0:
                        pe.wait_ge(act_lo_ready, TILES["mix1"] + j)
                    for b in range(2):
                        r = slice(64 * b, 64 * b + 64)
                        o = gemm_ps[3][r, t * P:(t + 1) * P]
                        nc.tensor.matmul(o, s_v[:, j // 4, t, r], s_pt[:, w % 2, 2 * b * P:(2 * b + 1) * P],
                                         start=True, stop=False)
                        mm = nc.tensor.matmul(o, s_v[0:64, j // 4, t + 1, r],
                                              s_pt[0:64, w % 2, (2 * b + 1) * P:(2 * b + 2) * P],
                                              start=False, stop=True)
                    mm.then_inc(so_ps, 1)

                steps = TT * 8
                gemm(pe, st, 1, 0, *B, None, banks=2)
                gemm(pe, st, 1, 1, *B, None, parts=(0, TT), banks=2)
                for w in range(steps + 3):
                    j = (w + 1) // TT + 1
                    if w < steps:
                        scores(w)
                    if j < 8:
                        gemm(pe, st, 1 + j // 4, j % 4, *B, None, parts=((w + 1) % TT, TT), banks=2)
                    if 2 <= w < steps + 2:
                        turn(w - 2)
                    if w >= 3:
                        output(w - 3)
                pe.wait_ge(spt_ready, steps)
                pe.wait_ge(act_lo_ready, TILES["mix1"] + 8)

            pe.wait_ge(og_ready, A_HEADS)
            plain(stages["EO"], A, TILES["mix0"], order=[4, 5, 6, 7, 0, 1, 2, 3])
            memory_products(0, 1, None)
            cross_attention(0, TILES["x1"])
            plain(stages["XO0"], A, TILES["att0"])
            ffn(0, TILES["x2"], 2)
            window_attention()
            plain(stages["SO"], A, TILES["mix1"])
            memory_products(1, 4, None)
            cross_attention(1, TILES["x4"])
            plain(stages["XO1"], A, TILES["att1"])
            ffn(1, TILES["x5"], 5)
            norm_sums(6)
            for q in range(2 * TT):
                t, hf = q // 2, q % 2
                pe.wait_ge(fin_scaled, 4 * hf + 4)
                wait(pe, fin_even if q % 2 == 0 else fin_odd, q // 2 - 1)
                for n in range(4):
                    mm = transpose(gemm_ps[q % 4][:, n * P:(n + 1) * P], x[:, 4 * hf + n, t * P:(t + 1) * P])
                mm.then_inc(fin_ps, 1)

        @block.scalar
        def _(act):
            for dst, src in param_rows:
                act.dma_start(dst, src).then_inc(params_in, 16)
            act.dma_start(ident[:, :], consts["ident"]).then_inc(consts_in, 16)
            act.dma_start(arena[:, 4096:4096 + 1408], consts["hgrn"]).then_inc(consts_in, 16)
            act.dma_start(s_dist[:, :, :], consts["dist"]).then_inc(consts_in, 16)
            act.dma_start(s_slope[:, :], consts["slope"]).then_inc(consts_in, 16)
            act.dma_start(sink8, a["swa_sinks"][0].partition_broadcast(P)).then_inc(consts_in, 16)

            def tile_out(n, m, parity, hi, ready, value):
                wait(act, sumsq_added, n + (8 * m - 1))
                act.wait_ge(ready, value)
                if hi is not None:
                    nc.scalar.activation(hi[:, n], x[:, n], ACT.Copy,
                                         scale=column(G_COLS[m], n)).then_inc(act_hi_ready, 1)
                nc.scalar.activation(sq[:, parity], x[:, n], ACT.Square).then_inc(sq_ready, 1)

            def norm_copy(n):
                act.wait_ge(norm_wide, n + 1)
                nc.scalar.activation(row_scale[:, :], aux_ps[2][:, :], ACT.Copy).then_inc(norm_ready, 1)

            st = stages["E"]
            act.wait_ge(vec_ready, 2)
            for n in range(KT):
                tile_out(n, 0, n % 2, a_hi, xt_taken, n + 1)
            act.wait_ge(lb_diff, 1)
            nc.scalar.activation(lb_e, lb_d, ACT.Exp).then_inc(lb_exp, 1)
            for slot in range(3):
                act.wait_ge(w_landed[slot], 16)
                nc.scalar.activation(w_hi[:, slot], w_raw[:, slot], ACT.Copy).then_inc(w_hi_ready, 1)

            def residual(stage, hi, m):
                def quad(i, last):
                    for j in range(4):
                        split_hi(act, stage, i, j)
                        if m is not None:
                            tile_out(i * 4 + j, m, j % 2, hi, block_taken, i * 4 + (stage.first + j + 1))

                run_quads(act, stage, quad)

            def conv_gates(i):
                for j in range(4):
                    split_hi(act, st, i, j)
                    if isinstance(i, int) and i == 0 and j == 0:
                        norm_copy(0)
                    if j % 2 == 0:
                        act.wait_ge(block_taken, i * 4 + (st.first + j + 1))
                        wait(act, gated, i * 2 + j // 2)
                        nc.scalar.activation(e_tanh, e_gate, ACT.Tanh, scale=0.5).then_inc(gate_tanh, 1)

            conv_gates(0)
            act.wait_ge(mem_in, 16)
            for m in range(MT):
                wait(act, mem_sq_ready, m)
                nc.scalar.activation(mem_sq, mem_tok[:, m], ACT.Square,
                                     accum_out=mem_ss[:, m:m + 1]).then_inc(mem_sq_ready, 1)
            conv_gates(1)
            act.wait_ge(mem_rstd, 1)
            for m in range(MT):
                nc.scalar.activation(mem_tok[:, m], mem_tok[:, m], ACT.Copy,
                                     scale=mem_rs[:, m:m + 1]).then_inc(mem_scaled, 1)
            for n in range(KT):
                act.wait_ge(memt_ps, n + 1)
                nc.scalar.activation(m_hi[:, n], aux_ps[n % 2][:, 0:N_MEM], ACT.Copy,
                                     scale=vec[:, V_MEM + n:V_MEM + n + 1]).then_inc(mem_hi, 1)
            with act.Fori(2, 5) as i:
                for j in range(4):
                    split_hi(act, st, i, j)
            for j in range(4):
                split_hi(act, st, 5, j)
                act.wait_ge(block_taken, st.first + 20 + j + 1)
                act.wait_ge(gated, 4 + j)
                nc.scalar.activation(e_tanh, e_gate, ACT.Tanh, scale=0.5).then_inc(gate_tanh, 1)

            act.wait_ge(neg_abs, 1)
            nc.scalar.activation(hg_k, hg_b, ACT.Tanh, scale=-0.5).then_inc(key_tanh, 1)
            nc.scalar.activation(pre_1, pre_1, ACT.Exp).then_inc(scalar_step, 1)
            for c in range(CT):
                act.wait_ge(centred, c + 1)
                nc.scalar.activation(ln_t[:, c], conv_y[:, c], ACT.Square).then_inc(cvar_sq, 1)
            act.wait_ge(lb_ready, 1)
            act.wait_ge(scalar_step, 1)
            nc.scalar.activation(pre_1, pre_1, ACT.Ln, bias=1.0).then_inc(log1p_a, 1)
            nc.scalar.activation(ln_rest, lb_rest, ACT.Ln).then_inc(lb_logs, 1)
            nc.scalar.activation(ln_scaled, lb_v, ACT.Ln, scale=2.0 ** 50).then_inc(lb_logs, 1)
            act.wait_ge(log_pair, 1)
            nc.scalar.activation(pre_2, pre_2, ACT.Exp).then_inc(scalar_step, 1)
            act.wait_ge(scalar_step, 2)
            nc.scalar.activation(pre_2, pre_2, ACT.Ln, bias=1.0).then_inc(log1p_b, 1)
            act.wait_ge(cvar_ps, 1)
            for c in range(CT):
                act.wait_ge(ln_out, c + 1)
                nc.scalar.activation(ln_t[:, c], conv_y[:, c], ACT.Tanh).then_inc(ln_tanh, 1)
            for c in range(CT):
                act.wait_ge(ln_act, c + 1)
                nc.scalar.activation(a_hi[:, 4 + c], conv_y[:, c], ACT.Copy).then_inc(act_hi_ready, 1)

            def head_square(h):
                act.wait_ge(o_ps, h + 1)
                nc.scalar.activation(hg_sq, by_chunk(gemm_ps[3][:, :]), ACT.Square).then_inc(o_sq, 1)

            def head_hi(h):
                act.wait_ge(og_ready, h + 1)
                nc.scalar.activation(a_hi[:, h], hg_out, ACT.Copy).then_inc(act_hi_ready, 1)

            def head(h, first):
                def level(n):
                    act.wait_ge(e_arg, h * 8 + (n + 2))
                    halves = hg_e[:, (n + 1) % 4].rearrange("p (b s w) -> p s b w", s=2, w=LEVELS[n])
                    nc.scalar.activation(halves[:, 0], halves[:, 0], ACT.Exp, scale=-1.0)
                    nc.scalar.activation(halves[:, 1], halves[:, 1], ACT.Exp).then_inc(e_exp, 1)

                act.wait_ge(e_arg, h * 8 + 1)
                nc.scalar.activation(hg_e[:, 0], hg_e[:, 0], ACT.Exp).then_inc(e_exp, 1)
                level(0)
                if not first:
                    head_square(h - 1)
                act.wait_ge(vt_ps, h + 1)
                nc.scalar.activation(hg_v_tok, by_chunk(gemm_ps[1][:, :]), ACT.Copy).then_inc(vt_ready, 1)
                act.wait_ge(kdt_ps, h + 1)
                nc.scalar.activation(hg_kd_tok, by_chunk(gemm_ps[0][:, 0:3 * P]), ACT.Copy).then_inc(kdt_ready, 1)
                level(1)
                nc.scalar.activation(hg_qe, hg_b[:, h], ACT.Exp).then_inc(qe_exp, 1)
                if not first:
                    act.wait_ge(st_ready, h * 3)
                nc.scalar.activation(edge, hg_b[:, h, P - 1::P], ACT.Exp).then_inc(edge_ready, 1)
                level(2)
                level(3)
                if not first:
                    head_hi(h - 1)
                for n in range(4, len(LEVELS)):
                    level(n)

            head(0, True)
            with act.Fori(1, A_HEADS) as h:
                head(h, False)
            head_square(A_HEADS - 1)
            head_hi(A_HEADS - 1)

            residual(stages["EO"], b_hi, 1)

            def memory_products(layer, n):
                st = stages[f"KV{layer}"]
                for at in range(8):
                    split_hi(act, st, at // 4, at % 4)
                    if at == 6:
                        norm_copy(n)
                for i in range(2, 4):
                    for j in range(4):
                        split_hi(act, st, i, j)
                        if j:
                            value_tile(layer, i, j - 1)
                    value_tile(layer, i, 3)

            def value_tile(layer, i, j):
                at = 4 * (i - 2) + j
                act.wait_ge(vf_turned, 8 * layer + at + 1)
                ps = by_chunk(aux_ps[j % 2][:, 0:MT * P])
                nc.scalar.activation(x_v[:, :, at * P:(at + 1) * P], ps, ACT.Copy).then_inc(vf_taken, 1)

            def cross_attention(layer):
                st = stages[f"XQ{layer}"]
                done = 4 * layer

                def softmax(h):
                    act.wait_ge(xs_max, done + h + 1)
                    wait(act, xpt_ps, done + h)
                    for t in range(TT):
                        mm = nc.scalar.activation(x_p[:, t], aux_ps[t // 2][:, (t % 2) * N_MEM:(t % 2 + 1) * N_MEM],
                                                  ACT.Exp, bias=xs_negmax[:, t:t + 1], accum_out=xs_sum[:, t:t + 1])
                    mm.then_inc(xs_exp, 1)

                def turned(h):
                    act.wait_ge(xpt_ps, done + h + 1)
                    wait(act, xo_ps, 2 * (done + h))
                    for m in range(MT):
                        mm = nc.scalar.activation(x_pt[:, m], aux_ps[2 + m][:, :], ACT.Copy)
                    mm.then_inc(xpt_ready, 1)

                def out_hi(h):
                    for d in range(2):
                        act.wait_ge(xo_ps, 2 * (done + h) + d + 1)
                        nc.scalar.activation(a_hi[:, 2 * h + d], aux_ps[2 + d][:, :], ACT.Copy).then_inc(act_hi_ready, 1)

                for h in range(X_HEADS + 2):
                    if h < X_HEADS:
                        split_hi(act, st, h // 2, 2 * (h % 2))
                    if h >= 2:
                        out_hi(h - 2)
                    if 1 <= h <= X_HEADS:
                        softmax(h - 1)
                    if h < X_HEADS:
                        split_hi(act, st, h // 2, 2 * (h % 2) + 1)
                    if 1 <= h <= X_HEADS:
                        turned(h - 1)

            def ffn(layer, n):
                for grp in range(3):
                    st = stages[f"FI{layer}{grp}"]
                    done = 22 * layer + 8 * grp

                    def quad(i, last):
                        for j in range(4):
                            split_hi(act, st, i, j)
                            if isinstance(i, int) and i == 0 and grp == 0 and j == 0:
                                norm_copy(n)
                            tile = i * 2 + (done + j // 2)
                            act.wait_ge(block_taken, i * 4 + (st.first + j + 1))
                            if j % 2 == 0:
                                wait(act, f_silu_ready, tile * 2 - 2)
                                nc.scalar.activation(f_tanh[:, j // 2], f_gate[:, j // 2], ACT.Tanh,
                                                     scale=0.5).then_inc(f_tanh_ready, 1)
                            else:
                                nc.scalar.activation(a_hi[:, i * 2 + j // 2], f_act[:, j // 2],
                                                     ACT.Copy).then_inc(act_hi_ready, 1)

                    if grp == 0:
                        quad(0, False)
                        with act.Fori(1, st.quads) as i:
                            quad(i, False)
                    else:
                        with act.Fori(0, st.quads) as i:
                            quad(i, False)
                    final = grp == 2
                    hi = b_hi if final and layer == 0 else None
                    residual(stages[f"FO{layer}{grp}"], hi, (3 if layer == 0 else 6) if final else None)

            def window_attention():
                st = stages["QKV"]
                for j in range(4):
                    split_hi(act, st, 0, j)
                    if j == 0:
                        norm_copy(3)
                for q in range(10):
                    n, m = q // 5, q % 5
                    rows = 64 if m == 4 else P
                    act.wait_ge(sv_ps, q + 1)
                    nc.scalar.activation(s_v[0:rows, n, m], aux_ps[q % 2][0:rows, 0:P], ACT.Copy).then_inc(sv_ready, 1)

                def softmax(w):
                    act.wait_ge(ss_max, w + 1)
                    wait(act, ss_norm, w - 1)
                    for b in range(2):
                        mm = nc.scalar.activation(s_e[:, w % 2, b], s_s[:, w % 2, b], ACT.Exp,
                                                  bias=ss_negmax[:, w % 2, b:b + 1], scale=C_HD ** -0.5,
                                                  accum_out=ss_sum[:, w % 2, b:b + 1])
                    mm.then_inc(ss_exp, 1)

                def turned(w):
                    act.wait_ge(spt_ps, w + 1)
                    wait(act, so_ps, w - 1)
                    src = gemm_ps[2][:, :].rearrange("p (b m q) -> p m b q", b=2, m=2)
                    dst = s_pt[:, w % 2].rearrange("p (b m q) -> p m b q", b=2, m=2)
                    nc.scalar.activation(dst[:, 0], src[:, 0], ACT.Copy)
                    nc.scalar.activation(dst[0:64, 1], src[0:64, 1], ACT.Copy).then_inc(spt_ready, 1)

                def out_hi(j):
                    act.wait_ge(so_ps, TT * (j + 1))
                    nc.scalar.activation(a_hi[:, j], gemm_ps[3][:, :], ACT.Copy).then_inc(act_hi_ready, 1)

                split_hi(act, st, 1, 0)
                split_hi(act, st, 1, 1)
                for w in range(TT * 8 + 3):
                    j = (w + 1) // TT + 1
                    if j < 8 and w % TT == TT - 1:
                        split_hi(act, st, 1 + j // 4, j % 4)
                    if w < TT * 8:
                        softmax(w)
                    if 2 <= w < TT * 8 + 2:
                        turned(w - 2)
                    if w >= 3 and (w - 3) % TT == TT - 1:
                        out_hi((w - 3) // TT)

            memory_products(0, 1)
            cross_attention(0)
            residual(stages["XO0"], b_hi, 2)
            ffn(0, 2)
            window_attention()
            residual(stages["SO"], b_hi, 4)
            memory_products(1, 4)
            cross_attention(1)
            residual(stages["XO1"], b_hi, 5)
            ffn(1, 5)
            act.wait_ge(norm_rstd, 7)
            for q in range(1, 2 * TT, 2):
                t = q // 2
                act.wait_ge(fin_ps, q + 1)
                nc.scalar.activation(o_tok[:, t, 512:1024], gemm_ps[q % 4][:, :], ACT.Copy,
                                     scale=rstd[:, t:t + 1]).then_inc(fin_odd, 1)

        @block.vector
        def _(dve):
            steps = [0]
            tt, ts, stt = nc.vector.tensor_tensor, nc.vector.tensor_scalar, nc.vector.scalar_tensor_tensor

            def step(ins):
                ins.then_inc(vector_step, 1)
                steps[0] += 1

            def settle(behind=0):
                wait(dve, vector_step, steps[0] - behind)

            dve.wait_ge(vec_turned, 1)
            nc.vector.tensor_copy(vec[:, :], aux_ps[0][:, 0:V_ROWS]).then_inc(vec_ready, 1)
            nc.vector.tensor_copy(conv_w[:, 0:B_KW * CT], aux_ps[0][:, P:P + B_KW * CT]).then_inc(vec_ready, 1)
            dve.wait_ge(vec_ready, 2)
            ts(onorm_half, vec[:, V_ONORM:V_ONORM + A_HEADS], 0.5 * P ** -0.5, None, ALU.mult)
            ts(lng_half, vec[:, V_LNG:V_LNG + CT], 0.5, None, ALU.mult)
            ts(lnb_half, vec[:, V_LNB:V_LNB + CT], 0.5, None, ALU.mult)
            dve.wait_ge(consts_in, 16 * 5)
            ts(sink8, sink8, C_HD ** 0.5, None, ALU.mult)
            tt(lb_d, vec[:, V_LB:V_LB + A_HEADS], vec[:, V_LB:V_LB + A_HEADS], ALU.subtract).then_inc(lb_diff, 1)

            def tile_lo(n, m, hi, lo, tiles):
                dve.wait_ge(act_hi_ready, n + (tiles + 1))
                stt(lo[:, n], x[:, n], column(G_COLS[m], n), hi[:, n].bitcast(F32), ALU.mult,
                    ALU.subtract).then_inc(act_lo_ready, 1)

            for n in range(KT + 1):
                if n < KT:
                    dve.wait_ge(xt_done, n + 1)
                    nc.vector.tensor_copy(x[:, n], gemm_ps[n % 4][:, :]).then_inc(xt_taken, 1)
                if n:
                    tile_lo(n - 1, 0, a_hi, a_lo, TILES["x0"])
            for slot in range(3):
                dve.wait_ge(w_hi_ready, slot + 1)
                tt(w_lo[:, slot], w_raw[:, slot], w_hi[:, slot].bitcast(F32), ALU.subtract).then_inc(w_lo_ready, 1)

            dve.wait_ge(lb_exp, 1)
            step(nc.vector.reciprocal(lb_r, lb_e))
            settle()
            step(tt(lb_r, lb_e, lb_r, ALU.mult))
            settle()
            step(tt(lb_v, lb_r, lb_r, ALU.subtract))
            settle()
            step(ts(lb_v, lb_v, LB_FLOOR, 1.0 - 1e-6, ALU.max, ALU.min))
            settle()
            step(ts(lb_rest, lb_v, -1.0, 1.0, ALU.mult, ALU.add))
            settle()
            ts(lb_half, lb_rest, 0.5, None, ALU.mult).then_inc(lb_ready, 1)

            def spread(values, ready):
                tt(diag[:, :, :], ident[:, :].unsqueeze(1).to_broadcast([P, TT, P]),
                   values.unsqueeze(2).to_broadcast([P, TT, P]), ALU.mult).then_inc(ready, 1)

            def mean_squares(dst, ps, scale, ready):
                ts(dst, ps, scale, EPS, ALU.mult, ALU.add).then_inc(ready, 1)

            def norm_means(n):
                dve.wait_ge(norm_ps, n + 1)
                mean_squares(ms, aux_ps[3][:, 0:TT], 1.0 / D, norm_ms)

            def norm_diagonal(n):
                dve.wait_ge(norm_rstd, n + 1)
                wait(dve, norm_wide, n)
                spread(rstd, norm_diag)

            def norm_stats(n):
                norm_means(n)
                norm_diagonal(n)
                dve.wait_ge(norm_ready, n + 1)

            def scaled(dst, stage, i, j, factor=None, banks=4):
                dve.wait_ge(block_done, i * 4 + (stage.first + j + 1))
                if factor is None:
                    ins = tt(dst, gemm_ps[j % banks][:, :], row_scale[:, :], ALU.mult)
                else:
                    ins = stt(dst, gemm_ps[j % banks][:, :], factor, row_scale[:, :], ALU.mult, ALU.mult)
                ins.then_inc(block_taken, 1)
                return i * 4 + (stage.first + j + 1)

            st = stages["E"]
            norm_stats(0)
            for i in range(2):
                if i:
                    dve.wait_ge(mem_sq_ready, MT)
                    mean_squares(mem_m, mem_ss, 1.0 / D, mem_ms)
                for j in range(4):
                    c = 2 * i + j // 2
                    wait(dve, gated, c)
                    taken = scaled(e_half if j % 2 else e_gate, st, i, j, 0.5 if j % 2 else None)
                    split_lo(dve, st, i, j)
                    if j % 2:
                        dve.wait_ge(gate_tanh, c + 1)
                        dve.wait_ge(block_taken, taken)
                        stt(u_pad[:, c, PAD:], e_tanh, 1.0, e_half, ALU.add, ALU.mult).then_inc(gated, 1)
            for n in range(KT):
                dve.wait_ge(mem_hi, n + 1)
                stt(m_lo[:, n], aux_ps[n % 2][:, 0:N_MEM], vec[:, V_MEM + n:V_MEM + n + 1], m_hi[:, n].bitcast(F32),
                    ALU.mult, ALU.subtract).then_inc(mem_lo, 1)
            dve.wait_ge(pad_ready, 1)
            dve.wait_ge(gated, CT)

            def tap(c, k):
                return u_pad[:, c, k:k + SEQ], conv_w[:, CT * k:CT * k + CT].rearrange("p (c o) -> p c o", o=1)[:, c]

            def conv_taps(c, part):
                n = DVE_TAPS // 4
                y = conv_y[:, c]
                for k in range(part * n, part * n + n):
                    u, w = tap(c, k)
                    into = conv_b2 if k % 2 else y
                    if k >= 2:
                        settle(1)
                    if k == 0:
                        step(ts(into, u, w, column(V_CONVB, c), ALU.mult, ALU.add))
                    elif k == 1:
                        step(ts(into, u, w, None, ALU.mult))
                    else:
                        step(stt(into, u, w, into, ALU.mult, ALU.add))

            def conv_merge(c):
                y = conv_y[:, c]
                settle()
                step(tt(y, y, conv_b2, ALU.add))
                settle()
                dve.wait_ge(pool_conv, c + 1)
                tt(y, y, conv_p, ALU.add).then_inc(conv_merged, 1)

            PER_TILE = DVE_TAPS + 1
            base = steps[0]
            with dve.Fori(0, 3) as c:
                steps[0] = c * PER_TILE + base
                for j in range(4):
                    scaled(early[:, c, j], st, c + 2, j)
                    split_lo(dve, st, c + 2, j)
                    conv_taps(c, j)
                conv_merge(c)
            steps[0] = base + 3 * PER_TILE
            for j in range(4):
                dve.wait_ge(gated, 4 + j)
                taken = scaled(e_gate, st, 5, j)
                split_lo(dve, st, 5, j)
                dve.wait_ge(gate_tanh, 4 + j + 1)
                dve.wait_ge(block_taken, taken)
                stt(hg_g[:, j], e_tanh, 1.0, e_gate, ALU.add, ALU.mult).then_inc(gated, 1)
                conv_taps(3, j)
            conv_merge(3)

            dve.wait_ge(block_taken, st.first + 24)
            dve.wait_ge(conv_merged, CT)
            stt(pre_1, hg_b, -1.0, hg_b, ALU.mult, ALU.min).then_inc(neg_abs, 1)
            dve.wait_ge(mean_wide, 1)
            for c in range(CT):
                stt(conv_y[:, c], aux_ps[2][:, :], -1.0 / B_CH, conv_y[:, c], ALU.mult, ALU.add).then_inc(centred, 1)
            dve.wait_ge(log1p_a, 1)
            step(stt(pre_1, hg_b, 0.0, pre_1, ALU.min, ALU.subtract))
            dve.wait_ge(lb_logs, 2)
            step(ts(ln_lb, ln_scaled, -LN2_50, None, ALU.add))
            settle()
            dve.wait_ge(key_tanh, 1)
            for h in range(A_HEADS):
                step(ts(hg_b[:, h], pre_1[:, h], ln_rest[:, h:h + 1], ln_lb[:, h:h + 1], ALU.add, ALU.max))
                step(ts(pre_2[:, h], pre_1[:, h], ln_rest[:, h:h + 1], ln_lb[:, h:h + 1], ALU.add, ALU.min))
            settle()
            tt(pre_2, pre_2, hg_b, ALU.subtract).then_inc(log_pair, 1)
            dve.wait_ge(cvar_ps, 1)
            mean_squares(cvar_m, aux_ps[3][:, 0:TT], 1.0 / B_CH, cvar_ms)
            for h in range(A_HEADS):
                step(ts(hg_k[:, h], hg_k[:, h], lb_half[:, h:h + 1], lb_half[:, h:h + 1], ALU.mult, ALU.add))
            dve.wait_ge(cvar_rstd, 1)
            spread(cvar_r, cvar_diag)
            dve.wait_ge(log1p_b, 1)
            step(tt(pre_2, pre_2, hg_b, ALU.add))
            settle()
            for h in range(A_HEADS):
                ins = nc.vector.tensor_tensor_scan(hg_b[:, h], scan_mask, pre_2[:, h], 0.0, ALU.mult, ALU.add)
            ins.then_inc(gates_ready, 1)
            dve.wait_ge(cvar_wide, 1)
            dve.wait_ge(centred, CT)
            for c in range(CT):
                step(tt(conv_y[:, c], conv_y[:, c], aux_ps[3][:, :], ALU.mult))
            for c in range(CT):
                settle(CT - 1 - c)
                ts(conv_y[:, c], conv_y[:, c], lng_half[:, c:c + 1], lnb_half[:, c:c + 1], ALU.mult,
                   ALU.add).then_inc(ln_out, 1)
            for c in range(CT):
                dve.wait_ge(ln_tanh, c + 1)
                stt(conv_y[:, c], ln_t[:, c], 1.0, conv_y[:, c], ALU.add, ALU.mult).then_inc(ln_act, 1)
            for c in range(CT):
                dve.wait_ge(act_hi_ready, TILES["mix0"] + c + 1)
                tt(a_lo[:, 4 + c], conv_y[:, c], a_hi[:, 4 + c].bitcast(F32), ALU.subtract).then_inc(act_lo_ready, 1)
            dve.wait_ge(gates_ready, 1)

            def bcast(ap, n):
                return ap.to_broadcast([P, TT, n])

            def head_mean_squares(h):
                dve.wait_ge(o_sq, h + 1)
                step(nc.vector.tensor_reduce(o_m, hg_sq, AX_X, ALU.add))
                settle()
                mean_squares(o_m, o_m, 1.0 / (P * P), o_ms)

            def head_norm(h):
                dve.wait_ge(o_rstd, h + 1)
                tt(hg_on, by_chunk(gemm_ps[3][:, :]), bcast(o_r.unsqueeze(2), P), ALU.mult).then_inc(on_ready, 1)

            def head_gate(h):
                dve.wait_ge(ont_ps, h + 1)
                stt(hg_out, aux_ps[2][:, :], onorm_half[:, h:h + 1], hg_g[:, h], ALU.mult,
                    ALU.mult).then_inc(og_ready, 1)

            def head_lo(h):
                dve.wait_ge(act_hi_ready, TILES["mix0"] + CT + h + 1)
                tt(a_lo[:, h], hg_out, a_hi[:, h].bitcast(F32), ALU.subtract).then_inc(act_lo_ready, 1)

            for h in range(A_HEADS):
                def level_product(n):
                    dve.wait_ge(e_exp, h * 8 + (n + 2))
                    wait(dve, lev_ps, h * 8 + n)
                    size = LEVELS[n]
                    e = hg_e[:, (n + 1) % 4].rearrange("p (b s w) -> p s b w", s=2, w=size)
                    qk = hg_qk[:, n % 2].rearrange("p (b s w) -> p s b w", s=2, w=size)
                    for s_, src in ((0, hg_k), (1, hg_q)):
                        v = src[:, h].rearrange("p (b s w) -> p s b w", s=2, w=size)[:, s_]
                        ins = tt(qk[:, s_], e[:, s_], v, ALU.mult)
                    ins.then_inc(lev_ready, 1)

                def level_take(n):
                    dve.wait_ge(lev_ps, h * 8 + (n + 2))
                    if n < 0:
                        wait(dve, o_ps, h)
                        tt(hg_scores, by_chunk(aux_ps[0][:, :]), ident[:, :].unsqueeze(1).to_broadcast([P, TT, P]),
                           ALU.mult).then_inc(lev_taken, 1)
                    else:
                        dve.wait_ge(lev_taken, h * 8 + (n + 1))
                        mask = lev_mask[:, n].bitcast(U32).unsqueeze(1).to_broadcast([P, TT, P])
                        nc.vector.copy_predicated(hg_scores, mask, by_chunk(aux_ps[(n + 1) % 2][:, :])).then_inc(lev_taken, 1)

                dve.wait_ge(e_exp, h * 8 + 1)
                tt(hg_e[:, 0], hg_e[:, 0], hg_k[:, h], ALU.mult).then_inc(kd_ready, 1)
                level_product(0)
                if h:
                    head_mean_squares(h - 1)
                level_take(-1)
                level_product(1)
                level_take(0)
                dve.wait_ge(qe_exp, h + 1)
                tt(hg_qe, hg_qe, hg_q[:, h], ALU.mult).then_inc(qe_ready, 1)
                dve.wait_ge(st_ps, h + 1)
                dve.wait_ge(edge_ready, h + 1)
                for c in range(3):
                    ps = gemm_ps[2][:, c * P:(c + 1) * P]
                    if c == 0:
                        nc.vector.tensor_copy(hg_state[:, 0], ps).then_inc(st_ready, 1)
                    else:
                        dve.wait_ge(st_ready, h * 3 + c)
                        stt(hg_state[:, c], hg_state[:, c - 1], edge[:, c:c + 1], ps, ALU.mult,
                            ALU.add).then_inc(st_ready, 1)
                for n in range(2, len(LEVELS)):
                    if h and n == 2:
                        head_norm(h - 1)
                    level_product(n)
                    level_take(n - 1)
                    if h and n == 2:
                        head_gate(h - 1)
                    if h and n == 3:
                        head_lo(h - 1)
                level_take(len(LEVELS) - 1)
            head_mean_squares(A_HEADS - 1)
            head_norm(A_HEADS - 1)
            head_gate(A_HEADS - 1)
            head_lo(A_HEADS - 1)

            def residual(stage, hi, lo, m, tiles, bias=None):
                def quad(i, last):
                    for j in range(4):
                        n = i * 4 + j
                        dve.wait_ge(block_done, i * 4 + (stage.first + j + 1))
                        if bias is None:
                            ins = tt(x[:, n], gemm_ps[j][:, :], x[:, n], ALU.add)
                        else:
                            ins = stt(x[:, n], gemm_ps[j][:, :], column(bias, n), x[:, n], ALU.add, ALU.add)
                        ins.then_inc(block_taken, 1)
                        split_lo(dve, stage, i, j)
                        if hi is not None:
                            tile_lo(n, m, hi, lo, tiles)

                run_quads(dve, stage, quad)

            residual(stages["EO"], b_hi, b_lo, 1, TILES["x1"])

            def memory_products(layer, n):
                st = stages[f"KV{layer}"]
                for i in range(4):
                    for j in range(4):
                        dve.wait_ge(block_done, st.first + 4 * i + j + 1)
                        if i < 2:
                            dst = x_k[:, 4 * i + j]
                        else:
                            wait(dve, vf_turned, 8 * layer + 4 * (i - 2) + j - 1)
                            dst = v_feat[:, j % 2]
                        nc.vector.tensor_copy(dst, gemm_ps[j][:, 0:N_MEM]).then_inc(block_taken, 1)
                        split_lo(dve, st, i, j)
                        at = 4 * i + j
                        if at == 1:
                            norm_means(n)
                        if at == 3:
                            norm_diagonal(n)
                        if at == 7:
                            dve.wait_ge(norm_ready, n + 1)

            def cross_attention(layer):
                st = stages[f"XQ{layer}"]
                done = 4 * layer
                tiles = TILES[f"att{layer}"]

                def query(h, d):
                    if d == 0:
                        wait(dve, xs_ps, done + h - 1)
                    scaled(x_q[:, h % 2, d], st, h // 2, 2 * (h % 2) + d, X_HD ** -0.5)
                    split_lo(dve, st, h // 2, 2 * (h % 2) + d)

                def out_lo(h):
                    for d in range(2):
                        dve.wait_ge(act_hi_ready, tiles + 2 * h + d + 1)
                        tt(a_lo[:, 2 * h + d], aux_ps[2 + d][:, :], a_hi[:, 2 * h + d].bitcast(F32),
                           ALU.subtract).then_inc(act_lo_ready, 1)

                def maxima(h):
                    dve.wait_ge(xs_ps, done + h + 1)
                    for b in range(2):
                        ps = aux_ps[b][:, :].rearrange("p (t m) -> p t m", m=N_MEM)
                        ins = nc.vector.tensor_reduce(xs_negmax[:, 2 * b:2 * b + 2], ps, AX_X, ALU.max, negate=True)
                    ins.then_inc(xs_max, 1)

                def normalise(h):
                    dve.wait_ge(xs_exp, done + h + 1)
                    step(nc.vector.reciprocal(xs_rec, xs_sum))
                    settle()
                    for t in range(TT):
                        ins = ts(x_p[:, t], x_p[:, t], xs_rec[:, t:t + 1], None, ALU.mult)
                    ins.then_inc(xs_norm, 1)

                for h in range(X_HEADS + 2):
                    if h < X_HEADS:
                        query(h, 0)
                    if h >= 2:
                        out_lo(h - 2)
                    if 1 <= h <= X_HEADS:
                        maxima(h - 1)
                    if h < X_HEADS:
                        query(h, 1)
                    if 1 <= h <= X_HEADS:
                        normalise(h - 1)

            def ffn(layer, n):
                for grp, size in enumerate(FF_GROUPS):
                    st = stages[f"FI{layer}{grp}"]
                    done = 22 * layer + 8 * grp
                    tiles = TILES[f"h{layer}{grp}"]

                    def quad(i):
                        for j in range(4):
                            s2 = j // 2
                            tile = i * 2 + (done + s2)
                            if j % 2 == 0:
                                wait(dve, f_silu_ready, tile * 2 - 2)
                                taken = scaled(f_gate[:, s2], st, i, j)
                                split_lo(dve, st, i, j)
                                dve.wait_ge(f_tanh_ready, tile + 1)
                                dve.wait_ge(block_taken, taken)
                                stt(f_silu[:, s2], f_tanh[:, s2], 1.0, f_gate[:, s2], ALU.add,
                                    ALU.mult).then_inc(f_silu_ready, 1)
                                dve.wait_ge(f_silu_ready, tile * 2 + 1)
                                stt(f_silu[:, s2], f_silu[:, s2], 0.5, row_scale[:, :], ALU.mult,
                                    ALU.mult).then_inc(f_silu_ready, 1)
                            else:
                                dve.wait_ge(block_done, i * 4 + (st.first + j + 1))
                                dve.wait_ge(f_silu_ready, tile * 2 + 2)
                                tt(f_act[:, s2], gemm_ps[j][:, :], f_silu[:, s2], ALU.mult).then_inc(block_taken, 1)
                                split_lo(dve, st, i, j)
                                dve.wait_ge(act_hi_ready, i * 2 + (tiles + s2 + 1))
                                tt(a_lo[:, i * 2 + s2], f_act[:, s2], a_hi[:, i * 2 + s2].bitcast(F32),
                                   ALU.subtract).then_inc(act_lo_ready, 1)

                    if grp == 0:
                        norm_stats(n)
                        quad(0)
                    with dve.Fori(1 if grp == 0 else 0, st.quads) as i:
                        quad(i)
                    so = stages[f"FO{layer}{grp}"]
                    if grp == 2 and layer == 0:
                        residual(so, b_hi, b_lo, 3, TILES["x3"])
                    else:
                        residual(so, None, None, None, None)

            def window_attention():
                st = stages["QKV"]
                norm_stats(3)
                for j in range(4):
                    dst = (s_k if j < 2 else s_vf)[:, j % 2, 64:]
                    taken = scaled(dst, st, 0, j)
                    dve.wait_ge(block_taken, taken)
                    ins = ts(dst, dst, vec[:, V_BKV + j:V_BKV + j + 1], None, ALU.add)
                    if j == 3:
                        ins.then_inc(sv_pad, 1)
                    split_lo(dve, st, 0, j)

                def query(j):
                    wait(dve, ss_ps, TT * (j - 1))
                    dst = s_q[:, j % 2]
                    taken = scaled(dst, st, 1 + j // 4, j % 4, banks=2)
                    dve.wait_ge(block_taken, taken)
                    ts(dst, dst, vec[:, V_BQ + j:V_BQ + j + 1], None, ALU.add).then_inc(sq_biased, 1)

                def scores(w):
                    j, t = w // TT, w % TT
                    dve.wait_ge(ss_ps, w + 1)
                    wait(dve, ss_exp, w - 1)
                    for b in range(2):
                        head = 8 * (j // 4) + j % 4 + 4 * b
                        stt(s_s[:, w % 2, b, 0:WIN], s_dist[:, 0 if t == 0 else 1], s_slope[:, head:head + 1],
                            aux_ps[2 * (w % 2) + b][:, 0:WIN], ALU.mult, ALU.add)
                    head = 8 * (j // 4) + j % 4
                    nc.vector.tensor_copy(s_s[:, w % 2, :, WIN], sink8[:, head:head + 5:4]).then_inc(ss_ready, 1)
                    dve.wait_ge(ss_ready, w + 1)
                    step(nc.vector.tensor_reduce(ss_negmax[:, w % 2], s_s[:, w % 2], AX_X, ALU.max))
                    settle()
                    ts(ss_negmax[:, w % 2], ss_negmax[:, w % 2], -C_HD ** -0.5, None, ALU.mult).then_inc(ss_max, 1)

                def normalise(w):
                    dve.wait_ge(ss_exp, w + 1)
                    step(nc.vector.reciprocal(ss_rec[:, w % 2], ss_sum[:, w % 2]))
                    settle()
                    wait(dve, spt_ps, w - 1)
                    for b in range(2):
                        ins = ts(s_p[:, w % 2, b], s_e[:, w % 2, b, 0:WIN], ss_rec[:, w % 2, b:b + 1], None, ALU.mult)
                    ins.then_inc(ss_norm, 1)

                def out_lo(j):
                    dve.wait_ge(act_hi_ready, TILES["mix1"] + j + 1)
                    tt(a_lo[:, j], gemm_ps[3][:, :], a_hi[:, j].bitcast(F32), ALU.subtract).then_inc(act_lo_ready, 1)

                split_lo(dve, st, 1, 0)
                query(0)
                split_lo(dve, st, 1, 1)
                for w in range(TT * 8 + 3):
                    j = w // TT + 1
                    if j < 8 and w % TT == TT - 1:
                        query(j)
                    if w >= TT + 3 and w % TT == TT - 1:
                        out_lo((w - 4) // TT)
                    if w < TT * 8:
                        scores(w)
                    if 1 <= w <= TT * 8:
                        normalise(w - 1)
                    if j < 7 and w % TT == TT - 1:
                        split_lo(dve, st, 1 + (j + 1) // 4, (j + 1) % 4)
                out_lo(7)

            memory_products(0, 1)
            cross_attention(0)
            residual(stages["XO0"], b_hi, b_lo, 2, TILES["x2"])
            ffn(0, 2)
            window_attention()
            residual(stages["SO"], b_hi, b_lo, 4, TILES["x4"], V_BO)
            memory_products(1, 4)
            cross_attention(1)
            residual(stages["XO1"], b_hi, b_lo, 5, TILES["x5"])
            ffn(1, 5)
            for n in range(KT):
                dve.wait_ge(sq_ready, 48 + n + 1)
                ts(x[:, n], x[:, n], vec[:, V_FINAL + n:V_FINAL + n + 1], None, ALU.mult).then_inc(fin_scaled, 1)
            dve.wait_ge(norm_ps, 7)
            mean_squares(ms, aux_ps[3][:, 0:TT], 1.0 / D, norm_ms)
            dve.wait_ge(norm_rstd, 7)
            for q in range(0, 2 * TT, 2):
                dve.wait_ge(fin_ps, q + 1)
                ts(o_tok[:, q // 2, 0:512], gemm_ps[q % 4][:, :], rstd[:, q // 2:q // 2 + 1], None,
                   ALU.mult).then_inc(fin_even, 1)

        @block.gpsimd
        def _(pool):
            def power(dst, src, n, ready):
                nc.gpsimd.tensor_tensor(dst, src, minus_half[:, 0:n], ALU.pow).then_inc(ready, 1)

            def clear_sums(n):
                nc.gpsimd.memset(sumsq[:, :], 0.0).then_inc(sumsq_clear, 1)
                pool.wait_ge(sumsq_clear, n + 1)

            nc.gpsimd.memset(ones[:, :], 1.0).then_inc(fills_ready, 1)
            nc.gpsimd.memset(minus_half[:, :], -0.5).then_inc(fills_ready, 1)
            pool.wait_ge(fills_ready, 2)

            def add_squares(m, n, parity):
                pool.wait_ge(sq_ready, n + (8 * m + 1))
                wait(pool, sumsq_added, n + 8 * m)
                nc.gpsimd.tensor_tensor(sumsq[:, :], sumsq[:, :], sq[:, parity], ALU.add).then_inc(sumsq_added, 1)

            def norm(m):
                if m:
                    pool.wait_ge(norm_ps, m)
                clear_sums(m)
                with pool.Fori(0, KT // 2) as i:
                    for j in range(2):
                        add_squares(m, i * 2 + j, j)

            def norm_power(m):
                pool.wait_ge(norm_ms, m + 1)
                wait(pool, norm_diag, m)
                power(rstd, ms, TT, norm_rstd)

            norm(0)
            norm_power(0)
            pool.wait_ge(xt_done, KT)
            nc.gpsimd.memset(u_pad[:, :, 0:PAD], 0.0).then_inc(pad_ready, 1)
            pool.wait_ge(mem_ms, 1)
            power(mem_rs, mem_m, MT, mem_rstd)
            pool.wait_ge(pad_ready, 1)
            pool.wait_ge(gated, CT)
            taps = list(range(DVE_TAPS, B_KW))
            per_tile = 2 * len(taps) - 1
            for c in range(CT):
                base = c * (per_tile - 1)
                wait(pool, conv_merged, c)
                count = 0
                for n, k in enumerate(taps):
                    u = u_pad[:, c, k:k + SEQ]
                    w = conv_w[:, CT * k:CT * k + CT].rearrange("p (c o) -> p c o", o=1)[:, c]
                    if n:
                        pool.wait_ge(pool_step, base + count)
                    nc.gpsimd.tensor_scalar(conv_pt if n else conv_p, u, w, None, ALU.mult).then_inc(pool_step, 1)
                    count += 1
                    if n:
                        pool.wait_ge(pool_step, base + count)
                        last = n == len(taps) - 1
                        nc.gpsimd.tensor_tensor(conv_p, conv_p, conv_pt, ALU.add).then_inc(
                            pool_conv if last else pool_step, 1)
                        count += not last
                assert count == per_tile - 1
            pool.wait_ge(cvar_ms, 1)
            power(cvar_r, cvar_m, TT, cvar_rstd)
            pool.wait_ge(gates_ready, 1)
            for h in range(A_HEADS):
                wait(pool, lev_ready, h * 7 - 3)
                b3 = by_chunk(hg_b[:, h])
                nc.gpsimd.tensor_tensor(by_chunk(hg_e[:, 0]), b3[:, :, P - 1:P].to_broadcast([P, TT, P]), b3,
                                        ALU.subtract).then_inc(e_arg, 1)
                for n, size in enumerate(LEVELS):
                    if n < 3:
                        wait(pool, lev_ready, h * 7 + n - 2)
                    elif n == 3:
                        pool.wait_ge(kdt_ps, h + 1)
                    else:
                        pool.wait_ge(lev_ready, h * 7 + n - 3)
                    b = hg_b[:, h].rearrange("p (b w) -> p b w", w=2 * size)
                    e = hg_e[:, (n + 1) % 4].rearrange("p (b w) -> p b w", w=2 * size)
                    mid = b[:, :, size - 1:size].to_broadcast([P, SEQ // (2 * size), 2 * size])
                    nc.gpsimd.tensor_tensor(e, b, mid, ALU.subtract).then_inc(e_arg, 1)
                    if h and n == 2:
                        pool.wait_ge(o_ms, h)
                        power(o_r, o_m, TT, o_rstd)
            pool.wait_ge(o_ms, A_HEADS)
            power(o_r, o_m, TT, o_rstd)
            norm(1)
            norm_power(1)
            norm(2)
            norm_power(2)
            norm(3)
            norm_power(3)
            pool.wait_ge(block_done, stages["QKV"].first)
            nc.gpsimd.memset(s_k[:, :, 0:64], 0.0)
            nc.gpsimd.memset(s_vf[:, :, 0:64], 0.0).then_inc(sv_pad, 1)
            for m in range(4, 7):
                norm(m)
                norm_power(m)


IN = ["x", "mem", "norm_mix", "norm_xattn", "norm_ffn", "norm_mem", "norm_final", "even_w_in", "even_w_out",
      "hgrn_lb_logits", "hgrn_out_norm", "conv_w", "conv_b", "conv_ln_g", "conv_ln_b", "swa_w_qkv", "swa_b_qkv",
      "swa_sinks", "swa_w_o", "swa_b_o", "xattn_w_q", "xattn_w_kv", "xattn_w_o", "ffn_w_in", "ffn_w_out"]


def shape_constants():
    ident = np.eye(P, dtype=np.float32)
    scan = np.ones(SEQ, np.float32)
    scan[::P] = 0
    s, t = np.arange(P)[:, None], np.arange(P)[None, :]
    masks = [((s // (2 * w) == t // (2 * w)) & (s % (2 * w) < w) & (t % (2 * w) >= w)) for w in LEVELS]
    hgrn = np.concatenate([np.broadcast_to(scan, (P, SEQ))] + [m.astype(np.float32) for m in masks], axis=1)
    r, c = np.arange(P)[:, None], np.arange(WIN)[None, :]
    inside = np.where(r < CHUNK, c < 2 * CHUNK, c >= CHUNK)
    first = inside & (c >= CHUNK)
    dist = np.stack([np.where(m, -np.abs(r + CHUNK - c).astype(np.float32), np.float32(-1e33)) for m in (first, inside)], 1)
    slope = np.broadcast_to((2.0 ** (-8.0 * np.arange(1, C_QH + 1) / C_QH) * C_HD ** 0.5).astype(np.float32), (P, C_QH))
    return {"ident": ident, "hgrn": np.ascontiguousarray(hgrn, np.float32),
            "dist": np.ascontiguousarray(dist, np.float32), "slope": np.ascontiguousarray(slope)}


def kernel(**inputs):
    import concourse.bacc as bacc
    from concourse.bass_utils import run_bass_kernel_spmd

    nc = bacc.Bacc("TRN2", target_bir_lowering=False, num_devices=1)
    arrays, aps = {}, {}
    for name in IN:
        v = np.ascontiguousarray(inputs[name])
        arrays["in_" + name] = v
        aps[name] = nc.dram_tensor("in_" + name, v.shape, mybir.dt.from_np(v.dtype), kind="ExternalInput").ap()
    consts = {}
    for name, v in shape_constants().items():
        arrays["const_" + name] = v
        consts[name] = nc.dram_tensor("const_" + name, v.shape, F32, kind="ExternalInput").ap()
    out = nc.dram_tensor("out", (1, SEQ, D), F32, kind="ExternalOutput").ap()
    trunk_kernel(nc, aps, consts, out)
    r = run_bass_kernel_spmd(nc, [arrays], core_ids=[0])
    return r.results[0]["out"]
```

```python
from contextlib import ExitStack

import numpy as np

import concourse.bass as bass
from concourse import mybir

F32 = mybir.dt.float32
F32R = mybir.dt.float32r
U32 = mybir.dt.uint32
ALU = mybir.AluOpType
ACT = mybir.ActivationFunctionType
AX_X = mybir.AxisListType.X

P = 128
D = 1024
SEQ = 512
N_MEM = 256
KT = D // P
TT = SEQ // P
MT = N_MEM // P
EPS = 1e-6
LB_FLOOR = 1e-30
A_HEADS = 4
B_CH = 512
CT = B_CH // P
B_KW = 31
PAD = B_KW - 1
DVE_TAPS = 16
POOL_TAPS = B_KW - DVE_TAPS
BLOCK_TAPS = (5, 5, 5, 5, 3, 3, 2, 3, 4, 4, 4, 4, 4, 4, 5, 4)
BLOCK_PRODUCTS = 4
CHUNK = 64
C_QH = 16
C_HD = 64
WIN = 192
X_HEADS = 4
X_HD = 256
HIDDEN = 2816
FF_GROUPS = (8, 8, 6)
LEVELS = (64, 32, 16, 8, 4, 2, 1)
LN2_50 = 50.0 * float(np.log(2.0))

V_MIX, V_XATTN, V_FFN, V_MEM, V_FINAL = 0, 16, 32, 48, 56
V_LB, V_ONORM, V_CONVB, V_LNG, V_LNB = 64, 68, 72, 76, 80
V_BQ, V_BKV, V_BO = 84, 92, 96
V_ROWS = 104


class Stage:

    def __init__(self, name, quads, kt, width, dmas):
        self.name, self.quads, self.kt, self.width, self.dmas = name, quads, kt, width, dmas
        self.first = 0
        self.landed = 0
        self.next = None


def plan_stages():
    stages = [Stage("E", 6, 8, SEQ, 1), Stage("EO", 2, 8, SEQ, 1)]
    for layer in range(2):
        if layer:
            stages += [Stage("QKV", 3, 8, SEQ, 2), Stage("SO", 2, 8, SEQ, 4)]
        stages += [Stage(f"KV{layer}", 4, 8, N_MEM, 1), Stage(f"XQ{layer}", 2, 8, SEQ, 1),
                   Stage(f"XO{layer}", 2, 8, SEQ, 1)]
        for n, tiles in enumerate(FF_GROUPS):
            stages += [Stage(f"FI{layer}{n}", tiles // 2, 8, SEQ, 1), Stage(f"FO{layer}{n}", 2, tiles, SEQ, 1)]
    first = landed = 0
    for s, after in zip(stages, stages[1:] + [None]):
        s.first, s.landed, s.next = first, landed, after
        first += 4 * s.quads
        landed += 16 * s.dmas * s.quads
    return {s.name: s for s in stages}


def trunk_kernel(nc, a, consts, out):
    stages = plan_stages()
    ctx = ExitStack()
    with ctx:
        def sb(name, shape, dt=F32):
            return ctx.enter_context(nc.sbuf_tensor(name, [P, *shape], dt))

        def sem(name):
            return ctx.enter_context(nc.semaphore(name))

        x = sb("x", [KT, SEQ])
        a_hi, a_lo = sb("a_hi", [KT, SEQ], F32R), sb("a_lo", [KT, SEQ], F32R)
        b_at = nc.sbuf_base
        b_hi, b_lo = sb("b_hi", [KT, SEQ], F32R), sb("b_lo", [KT, SEQ], F32R)
        b_end = nc.sbuf_base
        w_raw = sb("w_raw", [4, KT, P])
        w_hi, w_lo = sb("w_hi", [4, KT, P], F32R), sb("w_lo", [4, KT, P], F32R)
        m_hi, m_lo = sb("m_hi", [KT, N_MEM], F32R), sb("m_lo", [KT, N_MEM], F32R)
        row_scale = sb("row_scale", [SEQ])
        sumsq = sb("sumsq", [SEQ])
        sq = sb("sq", [2, SEQ])
        eps = sb("eps", [1])
        ident = sb("ident", [P])
        ones = sb("ones", [P])
        vec = sb("vec", [V_ROWS])
        minus_half = sb("minus_half", [16])
        stat = sb("stat", [160])
        used = [0]

        def small(n):
            used[0] += n
            return stat[:, used[0] - n:used[0]]

        ms, rstd = small(TT), small(TT)
        o_m, o_r = small(TT), small(TT)
        mem_ss, mem_m, mem_rs = small(MT), small(MT), small(MT)
        xs_negmax, xs_sum, xs_rec = small(TT), small(TT), small(TT)
        ss_negmax, ss_sum, ss_rec = (small(4).rearrange("p (a b) -> p a b", a=2) for _ in range(3))
        lb_d, lb_e, lb_r, lb_v, lb_rest, lb_half = (small(A_HEADS) for _ in range(6))
        ln_rest, ln_scaled, ln_lb = (small(A_HEADS) for _ in range(3))
        edge = small(TT)
        onorm_half, lng_half, lnb_half = small(A_HEADS), small(CT), small(CT)
        sink8 = small(C_QH)
        s_dist, s_slope = sb("s_dist", [2, WIN]), sb("s_slope", [C_QH])
        arena_floats = (nc.sbuf_bytes_remaining - 64) // 4
        arena = sb("arena", [arena_floats])
        early = nc.alloc_sbuf_tensor_at("early", [P, 4, 4, SEQ], F32, offset=b_at)
        assert b_end - b_at >= 4 * 4 * SEQ * 4

        class Carve:
            def __init__(self, at=0):
                self.at = at

            def __call__(self, *shape):
                n = int(np.prod(shape))
                assert self.at + n <= arena_floats, (self.at + n, arena_floats)
                v = arena[:, self.at:self.at + n]
                self.at += n
                if len(shape) == 2:
                    v = v.rearrange("p (a b) -> p a b", a=shape[0])
                elif len(shape) == 3:
                    v = v.rearrange("p (a b c) -> p a b c", a=shape[0], b=shape[1])
                return v

        carve = Carve()
        conv_y = carve(CT, SEQ)
        hg_k = carve(A_HEADS, SEQ)
        scan_mask = carve(SEQ)
        lev_mask = carve(len(LEVELS), P)
        conv_w = carve(P)
        heads_at = carve.at
        u_pad = carve(CT, PAD + SEQ)
        conv_b2, conv_p, conv_pt = carve(SEQ), carve(2, SEQ), carve(3, SEQ)
        e_gate, e_tanh, e_half = carve(SEQ), carve(SEQ), carve(SEQ)
        carve = Carve(heads_at)
        hg_e, hg_qk = carve(4, SEQ), carve(2, SEQ)
        hg_scores, hg_qe = carve(TT, P), carve(SEQ)
        hg_kd_tok, hg_v_tok, hg_state = carve(3, P), carve(TT, P), carve(3, P)
        hg_sq, hg_on, hg_out = carve(TT, P), carve(TT, P), carve(SEQ)
        x_tok = Carve(heads_at)(TT, D)
        mem_tok, mem_sq = Carve(CT * SEQ)(MT, D), Carve(2 * P)(D)
        vec_rows = Carve(0)(2 * P)
        spare = nc.alloc_sbuf_tensor_at("spare", [P, 2, KT, SEQ], F32, offset=b_at - 2 * KT * SEQ * 4)
        gate_t, ln_t, ln_sq = spare[:, 1, 0:A_HEADS], spare[:, 0, A_HEADS:], spare[:, 1, A_HEADS:]
        hg_q, hg_b, hg_v, hg_g = (early[:, n] for n in range(4))
        pre_1, pre_2 = hg_v, hg_g
        carve = Carve()
        x_k, x_v = carve(KT, N_MEM), carve(MT, D)
        late_at = carve.at
        v_feat = carve(2, N_MEM)
        carve = Carve(late_at)
        x_q, x_p, x_pt = carve(2, 2, SEQ), carve(TT, N_MEM), carve(MT, SEQ)
        carve = Carve(late_at)
        f_gate, f_tanh, f_silu, f_act = carve(2, SEQ), carve(2, SEQ), carve(2, SEQ), carve(2, SEQ)
        carve = Carve()
        s_k, s_vf = carve(2, 64 + SEQ), carve(2, 64 + SEQ)
        s_v = carve(2, 5, P)
        s_q = carve(2, SEQ)
        s_s, s_e = carve(2, 2, WIN + 1), carve(2, 2, WIN + 1)
        s_p, s_pt = carve(2, 2, WIN), carve(2, SEQ)
        o_tok = Carve()(TT, D)

        gemm_ps = [ctx.enter_context(nc.psum_tensor(f"gemm_ps{n}", [P, SEQ], F32)) for n in range(4)]
        aux_ps = [ctx.enter_context(nc.psum_tensor(f"aux_ps{n}", [P, SEQ], F32)) for n in range(4)]

        ident_in, consts_in, params_in, x_in, mem_in, stored = (
            sem(n) for n in ("ident_in", "consts_in", "params_in", "x_in", "mem_in", "stored"))
        w_landed = [sem(f"w_landed{n}") for n in range(4)]
        w_hi_ready, w_lo_ready, block_done, block_taken = (
            sem(n) for n in ("w_hi_ready", "w_lo_ready", "block_done", "block_taken"))
        act_hi_ready, act_lo_ready = sem("act_hi_ready"), sem("act_lo_ready")
        sq_ready, sumsq_added, sumsq_clear, norm_wide, norm_log, norm_ready = (
            sem(n) for n in ("sq_ready", "sumsq_added", "sumsq_clear", "norm_wide", "norm_log", "norm_ready"))
        fills_ready, pad_ready, vec_turned, vec_ready, xt_done, xt_taken = (
            sem(n) for n in ("fills_ready", "pad_ready", "vec_turned", "vec_ready", "xt_done", "xt_taken"))
        vector_step = sem("vector_step")
        gate_tanh, gated, conv_product, conv_added, conv_merged = (
            sem(n) for n in ("gate_tanh", "gated", "conv_product", "conv_added", "conv_merged"))
        mean_wide, centred, cvar_sq, cvar_wide, cvar_log, cvar_ready, ln_out, ln_tanh, ln_act = (
            sem(n) for n in ("mean_wide", "centred", "cvar_sq", "cvar_wide", "cvar_log", "cvar_ready", "ln_out",
                             "ln_tanh", "ln_act"))
        lb_diff, lb_exp, lb_ready, lb_logs, neg_abs, key_tanh, log1p_a, log_pair, log1p_b, gates_ready = (
            sem(n) for n in ("lb_diff", "lb_exp", "lb_ready", "lb_logs", "neg_abs", "key_tanh", "log1p_a",
                             "log_pair", "log1p_b", "gates_ready"))
        scalar_step = sem("scalar_step")
        kd_ready, qe_exp, qe_ready, edge_ready, vt_ps, vt_ready, kdt_ps, kdt_ready = (
            sem(n) for n in ("kd_ready", "qe_exp", "qe_ready", "edge_ready", "vt_ps",
                             "vt_ready", "kdt_ps", "kdt_ready"))
        e_arg, e_exp, lev_ready, lev_ps, lev_taken, st_ps, st_ready = (
            sem(n) for n in ("e_arg", "e_exp", "lev_ready", "lev_ps", "lev_taken", "st_ps", "st_ready"))
        o_ps, o_sq, o_ms, o_rstd, on_ready, ont_ps, og_ready = (
            sem(n) for n in ("o_ps", "o_sq", "o_ms", "o_rstd", "on_ready", "ont_ps", "og_ready"))
        mem_sq_ready, mem_ms, mem_rstd, mem_scaled, memt_ps, mem_hi, mem_lo, vf_turned, vf_taken = (
            sem(n) for n in ("mem_sq_ready", "mem_ms", "mem_rstd", "mem_scaled", "memt_ps", "mem_hi", "mem_lo",
                             "vf_turned", "vf_taken"))
        xs_ps, xs_max, xs_exp, xs_norm, xpt_ps, xpt_ready, xo_ps = (
            sem(n) for n in ("xs_ps", "xs_max", "xs_exp", "xs_norm", "xpt_ps", "xpt_ready", "xo_ps"))
        f_tanh_ready, f_silu_ready = sem("f_tanh_ready"), sem("f_silu_ready")
        sv_pad, sv_ps, sv_ready, ss_ps, ss_ready, ss_max, ss_exp, ss_norm, spt_ps, spt_ready, so_ps = (
            sem(n) for n in ("sv_pad", "sv_ps", "sv_ready", "ss_ps", "ss_ready", "ss_max", "ss_exp", "ss_norm",
                             "spt_ps", "spt_ready", "so_ps"))
        sq_biased = sem("sq_biased")
        fin_sums, fin_ms, fin_rstd, fin_scaled, fin_ps, fin_even, fin_odd = (
            sem(n) for n in ("fin_sums", "fin_ms", "fin_rstd", "fin_scaled", "fin_ps", "fin_even", "fin_odd"))

        block = ctx.enter_context(nc.Block())

        def wait(eng, s, value):
            if not (isinstance(value, int) and value <= 0):
                eng.wait_ge(s, value)

        TILES = {}
        count = 0
        for name, n in [("x0", 8), ("mix0", 8), ("x1", 8), ("att0", 8), ("x2", 8), ("h00", 8), ("h01", 8), ("h02", 6),
                        ("x3", 8), ("mix1", 8), ("x4", 8), ("att1", 8), ("x5", 8), ("h10", 8), ("h11", 8), ("h12", 6)]:
            TILES[name] = count
            count += n
        G_COLS = [V_MIX, V_XATTN, V_FFN, V_MIX + 8, V_XATTN + 8, V_FFN + 8, V_FINAL]

        def run_quads(eng, stage, body, whole=False):
            n = stage.quads
            peel = whole or stage.next is None or stage.next.dmas != stage.dmas
            if n - peel > 0:
                with eng.Fori(0, n - peel) as i:
                    body(i, False)
            if peel:
                body(n - 1, True)

        def landed(stage, i, ahead):
            if ahead and isinstance(i, int) and i == stage.quads - 1:
                return None if stage.next is None else stage.next.landed + 16 * stage.next.dmas
            return (i + 1 + ahead) * (16 * stage.dmas) + stage.landed

        def split_hi(act, stage, i, j):
            g = i * 4 + (stage.first + j + 3)
            slot = (j + 3) % 4
            value = landed(stage, i, 0 if j == 0 else 1)
            if value is None:
                return
            act.wait_ge(w_landed[slot], value)
            wait(act, block_done, g - 3)
            nc.scalar.activation(w_hi[:, slot], w_raw[:, slot], ACT.Copy).then_inc(w_hi_ready, 1)

        def split_lo(dve, stage, i, j):
            g = i * 4 + (stage.first + j + 3)
            slot = (j + 3) % 4
            if landed(stage, i, 0 if j == 0 else 1) is None:
                return
            dve.wait_ge(w_hi_ready, g + 1)
            nc.vector.tensor_tensor(w_lo[:, slot], w_raw[:, slot], w_hi[:, slot].bitcast(F32),
                                    ALU.subtract).then_inc(w_lo_ready, 1)

        def gemm(pe, stage, i, j, hi, lo, tiles, order=None, parts=(0, 1), banks=4):
            g = i * 4 + (stage.first + j)
            order = order or list(range(stage.kt))
            width = stage.width
            start, stop = len(order) * parts[0] // parts[1], len(order) * (parts[0] + 1) // parts[1]
            if parts[1] == 1:
                start, stop = 0, len(order)
            if start == 0:
                pe.wait_ge(w_lo_ready, g + 1)
                wait(pe, block_taken, g + 1 - banks)
            for n in range(start, stop):
                k = order[n]
                if j == 0 and tiles is not None:
                    pe.wait_ge(act_lo_ready, tiles + n + 1)
                first, last = n == 0, n == len(order) - 1
                o = gemm_ps[j % banks][:, 0:width]
                nc.tensor.matmul(o, w_hi[:, j, k], hi[:, k, 0:width], start=first, stop=False)
                nc.tensor.matmul(o, w_hi[:, j, k], lo[:, k, 0:width], start=False, stop=False)
                mm = nc.tensor.matmul(o, w_lo[:, j, k], hi[:, k, 0:width], start=False, stop=last)
            if stop == len(order):
                mm.then_inc(block_done, 1)

        A, B = (a_hi, a_lo), (b_hi, b_lo)

        def column(first, n):
            return vec[:, :].rearrange("p (v o) -> p v o", o=1)[:, n + first]

        def by_chunk(ap):
            return ap.rearrange("p (c q) -> p c q", q=P)

        def rows(w, at):
            w = w.rearrange("(r p) -> r p", p=P)
            return vec_rows[at:at + w.shape[0], 0:P], w

        param_rows = [rows(a[name].rearrange("l d -> (l d)"), at) for name, at in [
            ("norm_mix", V_MIX), ("norm_xattn", V_XATTN), ("norm_ffn", V_FFN), ("hgrn_lb_logits", V_LB),
            ("conv_b", V_CONVB), ("conv_ln_g", V_LNG), ("conv_ln_b", V_LNB), ("swa_b_o", V_BO)]]
        param_rows += [rows(a["norm_mem"], V_MEM), rows(a["norm_final"], V_FINAL),
                       rows(a["hgrn_out_norm"].rearrange("l h d -> (l h d)"), V_ONORM),
                       rows(a["swa_b_qkv"][0, C_QH * C_HD:], V_BKV)]
        bq = a["swa_b_qkv"][0, 0:C_QH * C_HD].rearrange("(a b j d) -> a b j d", a=2, b=2, j=4)
        for i in range(2):
            for b in range(2):
                param_rows.append((vec_rows[V_BQ + 4 * i:V_BQ + 4 * i + 4, 64 * b:64 * b + 64], bq[i, b]))
        param_rows.append((vec_rows[0:B_KW * CT, P:2 * P], a["conv_w"][0].rearrange("k (c p) -> (k c) p", p=P)))

        @block.sync
        def _(sp):
            sp.dma_start(ident[:, :], consts["ident"]).then_inc(ident_in, 16)
            sp.dma_start(x_tok, a["x"][0].rearrange("(t p) d -> p t d", p=P)).then_inc(x_in, 16)
            for dst, src in param_rows:
                sp.dma_start(dst, src).then_inc(params_in, 16)

            def cols(w):
                return w.rearrange("(k p) (b n) -> b p k n", p=P, n=P)

            def load(stage, source, block_of):
                kt = stage.kt

                def quad(i, j):
                    g = i * 4 + (stage.first + j)
                    wait(sp, w_lo_ready, g - 3)
                    sp.dma_start(w_raw[:, j, 0:kt], source[block_of(i, j)]).then_inc(w_landed[j], 16)

                return quad

            def run(stage, quad, lo=0):
                hi = stage.quads
                if hi - lo > 1:
                    with sp.Fori(lo, hi) as i:
                        for j in range(4):
                            quad(i, j)
                elif hi > lo:
                    for j in range(4):
                        quad(lo, j)

            e = cols(a["even_w_in"][0])
            st = stages["E"]
            gg, ga = 2560 // P, 2048 // P
            quad = load(st, e, lambda i, j: i * 2 + ((ga if j % 2 else gg) + j // 2))
            for i in range(2):
                for j in range(4):
                    quad(i, j)
                if i == 0:
                    sp.dma_start(mem_tok, a["mem"][0].rearrange("(m p) d -> p m d", p=P)).then_inc(mem_in, 16)
                    sp.dma_start(sink8, a["swa_sinks"][0].partition_broadcast(P)).then_inc(consts_in, 16)
                    sp.dma_start(arena[:, 4096:4096 + 1408], consts["hgrn"]).then_inc(consts_in, 16)
                    sp.dma_start(s_dist[:, :, :], consts["dist"]).then_inc(consts_in, 16)
                    sp.dma_start(s_slope[:, :], consts["slope"]).then_inc(consts_in, 16)
            for i in (2, 3):
                for j in range(4):
                    load(st, e, lambda i, j: (3 - i) * 4 + j)(i, j)
            run(st, load(st, e, lambda i, j: i * 4 + (j - 8)), 4)

            def plain(name, w):
                run(stages[name], load(stages[name], cols(w), lambda i, j: i * 4 + j))

            def ffn(layer):
                w_in, w_out = a["ffn_w_in"][layer], a["ffn_w_out"][layer]
                at = 0
                for n, tiles in enumerate(FF_GROUPS):
                    st = stages[f"FI{layer}{n}"]
                    run(st, load(st, cols(w_in), lambda i, j, at=at: i * 2 + (at + j // 2 + (HIDDEN // P) * (j % 2))))
                    plain(f"FO{layer}{n}", w_out[at * P:(at + tiles) * P])
                    at += tiles

            plain("EO", a["even_w_out"][0])
            for layer in range(2):
                if layer:
                    wq = a["swa_w_qkv"][0].rearrange("(k p) (h d) -> h p k d", p=P, d=C_HD)
                    st = stages["QKV"]
                    for j in range(4):
                        sp.wait_ge(w_lo_ready, st.first + j - 3)
                        for b in range(2):
                            sp.dma_start(w_raw[:, j, :, b * 64:b * 64 + 64], wq[C_QH + 2 * j + b]).then_inc(w_landed[j], 16)
                    for i in range(2):
                        for j in range(4):
                            sp.wait_ge(w_lo_ready, st.first + 4 + 4 * i + j - 3)
                            for b in range(2):
                                sp.dma_start(w_raw[:, j, :, b * 64:b * 64 + 64],
                                             wq[8 * i + j + 4 * b]).then_inc(w_landed[j], 16)
                    wo = a["swa_w_o"][0].rearrange("(a b j d) (c n) -> c a b d j n", a=2, b=2, j=4, n=P)
                    st = stages["SO"]
                    with sp.Fori(0, 2) as i:
                        for j in range(4):
                            sp.wait_ge(w_lo_ready, i * 4 + (st.first + j - 3))
                            for half_ in range(2):
                                for b in range(2):
                                    sp.dma_start(w_raw[b * 64:b * 64 + 64, j, 4 * half_:4 * half_ + 4, :],
                                                 wo[i * 4 + j, half_, b]).then_inc(w_landed[j], 16)
                plain(f"KV{layer}", a["xattn_w_kv"][layer])
                plain(f"XQ{layer}", a["xattn_w_q"][layer])
                plain(f"XO{layer}", a["xattn_w_o"][layer])
                ffn(layer)
            o_rows = out[0].rearrange("(t p) d -> p t d", p=P)
            for t in range(TT):
                sp.wait_ge(fin_even, t + 1)
                sp.wait_ge(fin_odd, t + 1)
                sp.dma_start(o_rows[:, t], o_tok[:, t]).then_inc(stored, 16)
            sp.wait_ge(stored, 16 * TT)

        @block.tensor
        def _(pe):
            def transpose(o, i_, size=P):
                return nc.tensor.transpose(o, i_, ident[0:size, 0:size])

            pe.wait_ge(ident_in, 16)
            pe.wait_ge(params_in, 16 * len(param_rows))
            transpose(aux_ps[0][:, 0:V_ROWS], vec_rows[0:V_ROWS, 0:P], V_ROWS)
            transpose(aux_ps[0][:, P:P + B_KW * CT], vec_rows[0:B_KW * CT, P:2 * P],
                      B_KW * CT).then_inc(vec_turned, 1)

            def turn_input(n):
                wait(pe, xt_taken, n - 3)
                for t in range(TT):
                    mm = transpose(aux_ps[(n + 1) % 4][:, t * P:(t + 1) * P], x_tok[:, t, n * P:(n + 1) * P])
                mm.then_inc(xt_done, 1)

            def norm_sums(n):
                pe.wait_ge(sumsq_added, 8 * (n + 1))
                nc.tensor.matmul(aux_ps[2][:, :], ones[:, :], sumsq[:, :], start=True, stop=True).then_inc(norm_wide, 1)

            def first_quad(stage, inp, tiles, n, rest_of_input=False):
                if rest_of_input:
                    for k in range(KT):
                        gemm(pe, stage, 0, 0, *inp, tiles, parts=(k, KT))
                        if k + 6 < KT:
                            turn_input(k + 6)
                else:
                    gemm(pe, stage, 0, 0, *inp, tiles)
                norm_sums(n)
                gemm(pe, stage, 0, 1, *inp, tiles)
                gemm(pe, stage, 0, 2, *inp, tiles)
                gemm(pe, stage, 0, 3, *inp, tiles)

            def plain(stage, inp, tiles, lo=0, order=None):
                if stage.quads > lo:
                    with pe.Fori(lo, stage.quads) as i:
                        for j in range(4):
                            gemm(pe, stage, i, j, *inp, tiles, order)

            pe.wait_ge(x_in, 16)
            for n in range(6):
                if n == 3:
                    pe.wait_ge(vec_ready, 2)
                turn_input(n)
            first_quad(stages["E"], A, TILES["x0"], 0, rest_of_input=True)
            for j in range(4):
                gemm(pe, stages["E"], 1, j, *A, None)
            pe.wait_ge(mem_scaled, MT)
            for n in range(KT):
                if n % 2 == 0:
                    gemm(pe, stages["E"], 2, n // 2, *A, None)
                wait(pe, mem_lo, n - 1)
                for m in range(MT):
                    mm = transpose(aux_ps[n % 2][:, m * P:(m + 1) * P], mem_tok[:, m, n * P:(n + 1) * P])
                mm.then_inc(memt_ps, 1)
            plain(stages["E"], A, None, 3)

            for c in range(CT):
                pe.wait_ge(conv_merged, c + 1)
                mm = nc.tensor.matmul(aux_ps[2][:, :], ones[:, :], conv_y[:, c], start=c == 0, stop=c == CT - 1)
            mm.then_inc(mean_wide, 1)

            def conv_variance():
                for c in range(CT):
                    pe.wait_ge(cvar_sq, c + 1)
                    mm = nc.tensor.matmul(aux_ps[3][:, :], ones[:, :], ln_sq[:, c], start=c == 0, stop=c == CT - 1)
                mm.then_inc(cvar_wide, 1)

            def turn_outputs(h):
                pe.wait_ge(on_ready, h + 1)
                for c in range(TT):
                    mm = transpose(aux_ps[2][:, c * P:(c + 1) * P], hg_on[:, c])
                mm.then_inc(ont_ps, 1)

            for h in range(A_HEADS):
                wait(pe, vt_ready, h)
                for c in range(TT):
                    mm = transpose(gemm_ps[1][:, c * P:(c + 1) * P], hg_v[:, h, c * P:(c + 1) * P])
                mm.then_inc(vt_ps, 1)
                pe.wait_ge(gates_ready, 1)
                wait(pe, lev_taken, h * 8)
                for c in range(TT):
                    s = slice(c * P, (c + 1) * P)
                    mm = nc.tensor.matmul(aux_ps[0][:, s], hg_k[:, h, s], hg_q[:, h, s], start=True, stop=True)
                mm.then_inc(lev_ps, 1)
                pe.wait_ge(kd_ready, h + 1)
                wait(pe, kdt_ready, h)
                for c in range(3):
                    mm = transpose(gemm_ps[0][:, c * P:(c + 1) * P], hg_e[:, 0, c * P:(c + 1) * P])
                mm.then_inc(kdt_ps, 1)

                def level(n):
                    pe.wait_ge(lev_ready, h * 7 + (n + 1))
                    wait(pe, lev_taken, h * 8 + n)
                    for c in range(TT):
                        s = slice(c * P, (c + 1) * P)
                        qk = hg_qk[:, n % 2, s]
                        mm = nc.tensor.matmul(aux_ps[(n + 1) % 2][:, s], qk, qk, start=True, stop=True)
                    mm.then_inc(lev_ps, 1)

                level(0)
                pe.wait_ge(kdt_ready, h + 1)
                pe.wait_ge(vt_ready, h + 1)
                for c in range(3):
                    mm = nc.tensor.matmul(gemm_ps[2][:, c * P:(c + 1) * P], hg_kd_tok[:, c], hg_v_tok[:, c],
                                          start=True, stop=True)
                mm.then_inc(st_ps, 1)
                level(1)
                if h:
                    turn_outputs(h - 1)
                for n in range(2, len(LEVELS)):
                    level(n)
                    if h == 0 and n == len(LEVELS) - 1:
                        conv_variance()
                pe.wait_ge(lev_taken, h * 8 + 8)
                pe.wait_ge(st_ready, h * 3 + 3)
                pe.wait_ge(qe_ready, h + 1)
                for c in range(TT):
                    s = slice(c * P, (c + 1) * P)
                    mm = nc.tensor.matmul(gemm_ps[3][:, s], hg_scores[:, c], hg_v_tok[:, c], start=True, stop=c == 0)
                    if c:
                        mm = nc.tensor.matmul(gemm_ps[3][:, s], hg_qe[:, s], hg_state[:, c - 1], start=False, stop=True)
                mm.then_inc(o_ps, 1)
            so, tiles_out, order = stages["EO"], TILES["mix0"], [0, 4, 5, 6, 7, 1, 2, 3]
            for j in range(3):
                for k in range(KT - 1):
                    gemm(pe, so, 0, j, *A, tiles_out, order, parts=(k, KT))
                if j == 0:
                    turn_outputs(A_HEADS - 1)
            for j in range(3):
                gemm(pe, so, 0, j, *A, tiles_out, order, parts=(KT - 1, KT))
            gemm(pe, so, 0, 3, *A, None, order)
            plain(so, A, None, 1, order)

            def cross_attention(layer, tiles_in):
                st = stages[f"XQ{layer}"]
                inp = B
                done = 4 * layer

                def scores(h):
                    pe.wait_ge(block_taken, st.first + 2 * h + 2)
                    pe.wait_ge(xs_exp, done + h)
                    pe.wait_ge(vf_taken, 8 * layer + 8)
                    for t in range(TT):
                        for d in range(2):
                            mm = nc.tensor.matmul(aux_ps[t // 2][:, (t % 2) * N_MEM:(t % 2 + 1) * N_MEM],
                                                  x_q[:, h % 2, d, t * P:(t + 1) * P], x_k[:, 2 * h + d],
                                                  start=d == 0, stop=d == 1)
                    mm.then_inc(xs_ps, 1)

                def turn(h):
                    pe.wait_ge(xs_norm, done + h + 1)
                    pe.wait_ge(act_lo_ready, TILES[f"att{layer}"] + 2 * h)
                    for m in range(MT):
                        for t in range(TT):
                            mm = transpose(aux_ps[2 + m][:, t * P:(t + 1) * P], x_p[:, t, m * P:(m + 1) * P])
                    mm.then_inc(xpt_ps, 1)

                def output(h):
                    pe.wait_ge(xpt_ready, done + h + 1)
                    for d in range(2):
                        for m in range(MT):
                            col = h * X_HD + d * P
                            mm = nc.tensor.matmul(aux_ps[2 + d][:, :], x_v[:, m, col:col + P], x_pt[:, m],
                                                  start=m == 0, stop=m == MT - 1)
                        mm.then_inc(xo_ps, 1)

                for h in range(X_HEADS):
                    gemm(pe, st, h // 2, 2 * (h % 2), *inp, tiles_in if h == 0 else None)
                    if h >= 2:
                        output(h - 2)
                    if h:
                        scores(h - 1)
                    gemm(pe, st, h // 2, 2 * (h % 2) + 1, *inp, None)
                    if h:
                        turn(h - 1)
                so, tiles_out = stages[f"XO{layer}"], TILES[f"att{layer}"]
                output(X_HEADS - 2)
                scores(X_HEADS - 1)
                gemm(pe, so, 0, 0, *A, tiles_out, parts=(0, 2))
                gemm(pe, so, 0, 1, *A, None, parts=(0, 2))
                turn(X_HEADS - 1)
                gemm(pe, so, 0, 2, *A, None, parts=(0, 2))
                output(X_HEADS - 1)
                for j in range(3):
                    gemm(pe, so, 0, j, *A, tiles_out, parts=(1, 2))
                gemm(pe, so, 0, 3, *A, None)
                plain(so, A, None, 1)

            def memory_products(layer, n, tiles_in):
                st = stages[f"KV{layer}"]
                mem = (m_hi, m_lo)
                if layer == 0:
                    pe.wait_ge(mem_lo, KT)
                for at in range(8):
                    if at == 1:
                        norm_sums(n)
                    gemm(pe, st, at // 4, at % 4, *mem, None)

                def turn(i, j):
                    at = i * 4 + (8 * layer + j - 8)
                    pe.wait_ge(block_taken, i * 4 + (st.first + j + 1))
                    wait(pe, vf_taken, at - 1)
                    for m in range(MT):
                        mm = transpose(aux_ps[j % 2][:, m * P:(m + 1) * P], v_feat[:, j % 2, m * P:(m + 1) * P])
                    mm.then_inc(vf_turned, 1)

                for i in range(2, 4):
                    for j in range(4):
                        gemm(pe, st, i, j, *mem, None)
                        if j:
                            turn(i, j - 1)
                    turn(i, 3)

            def ffn(layer, tiles_in, n):
                for grp in range(3):
                    st, so = stages[f"FI{layer}{grp}"], stages[f"FO{layer}{grp}"]
                    if grp == 0:
                        first_quad(st, B, tiles_in, n)
                        plain(st, B, None, 1)
                    else:
                        plain(st, B, None)
                    plain(so, A, TILES[f"h{layer}{grp}"])

            def window_attention():
                st = stages["QKV"]
                first_quad(st, B, TILES["x3"], 3)
                pe.wait_ge(sv_pad, 2)
                for n in range(2):
                    for m in range(5):
                        rows = 64 if m == 4 else P
                        q = n * 5 + m
                        wait(pe, sv_ready, q - 1)
                        mm = transpose(aux_ps[q % 2][0:rows, 0:P], s_vf[:, n, m * P:m * P + rows])
                        mm.then_inc(sv_ps, 1)

                def scores(w):
                    j, t = w // TT, w % TT
                    pe.wait_ge(sq_biased, j + 1)
                    wait(pe, ss_ready, w - 1)
                    if w < 2:
                        pe.wait_ge(sv_ready, 10)
                    for b in range(2):
                        r = slice(64 * b, 64 * b + 64)
                        mm = nc.tensor.matmul(aux_ps[2 * (w % 2) + b][:, 0:WIN],
                                              s_q[r, j % 2, t * P:(t + 1) * P],
                                              s_k[r, j // 4, t * P:t * P + WIN], start=True, stop=True)
                    mm.then_inc(ss_ps, 1)

                def turn(w):
                    pe.wait_ge(ss_norm, w + 1)
                    wait(pe, spt_ready, w)
                    for b in range(2):
                        transpose(gemm_ps[2][:, 2 * b * P:(2 * b + 1) * P], s_p[:, w % 2, b, 0:P])
                        mm = transpose(gemm_ps[2][0:64, (2 * b + 1) * P:(2 * b + 2) * P], s_p[:, w % 2, b, P:WIN])
                    mm.then_inc(spt_ps, 1)

                def output(w):
                    j, t = w // TT, w % TT
                    pe.wait_ge(spt_ready, w + 1)
                    if t == 0:
                        pe.wait_ge(act_lo_ready, TILES["mix1"] + j)
                    for b in range(2):
                        r = slice(64 * b, 64 * b + 64)
                        o = gemm_ps[3][r, t * P:(t + 1) * P]
                        nc.tensor.matmul(o, s_v[:, j // 4, t, r], s_pt[:, w % 2, 2 * b * P:(2 * b + 1) * P],
                                         start=True, stop=False)
                        mm = nc.tensor.matmul(o, s_v[0:64, j // 4, t + 1, r],
                                              s_pt[0:64, w % 2, (2 * b + 1) * P:(2 * b + 2) * P],
                                              start=False, stop=True)
                    mm.then_inc(so_ps, 1)

                steps = TT * 8
                so, tiles_out = stages["SO"], TILES["mix1"]
                gemm(pe, st, 1, 0, *B, None, banks=2)
                gemm(pe, st, 1, 1, *B, None, parts=(0, TT), banks=2)
                for w in range(steps + 3):
                    j = (w + 1) // TT + 1
                    if w < steps:
                        scores(w)
                    if j < 8:
                        gemm(pe, st, 1 + j // 4, j % 4, *B, None, parts=((w + 1) % TT, TT), banks=2)
                    if steps - 4 <= w < steps + 2:
                        gemm(pe, so, 0, w % 2, *A, tiles_out, parts=((w - steps + 4) // 2, 4), banks=2)
                    if 2 <= w < steps + 2:
                        turn(w - 2)
                    if w >= 3:
                        output(w - 3)
                for j in range(2):
                    gemm(pe, so, 0, j, *A, tiles_out, parts=(3, 4), banks=2)
                pe.wait_ge(spt_ready, steps)
                pe.wait_ge(act_lo_ready, tiles_out + 8)
                gemm(pe, so, 0, 2, *A, None)
                gemm(pe, so, 0, 3, *A, None)
                plain(so, A, None, 1)

            memory_products(0, 1, None)
            cross_attention(0, TILES["x1"])
            ffn(0, TILES["x2"], 2)
            window_attention()
            memory_products(1, 4, None)
            cross_attention(1, TILES["x4"])
            ffn(1, TILES["x5"], 5)
            pe.wait_ge(sumsq_added, 8 * 7)
            for t in range(TT):
                mm = nc.tensor.matmul(aux_ps[3][:, t:t + 1], sumsq[:, t * P:(t + 1) * P], ones[:, 0:1],
                                      start=True, stop=True)
            mm.then_inc(fin_sums, 1)
            for q in range(2 * TT):
                t, hf = q // 2, q % 2
                pe.wait_ge(fin_scaled, 4 * hf + 4)
                wait(pe, fin_even if q % 2 == 0 else fin_odd, q // 2 - 1)
                for n in range(4):
                    mm = transpose(gemm_ps[q % 4][:, n * P:(n + 1) * P], x[:, 4 * hf + n, t * P:(t + 1) * P])
                mm.then_inc(fin_ps, 1)

        @block.scalar
        def _(act):
            def tile_out(n, m, parity, hi, ready, value):
                wait(act, sumsq_added, n + (8 * m - 1))
                act.wait_ge(ready, value)
                if hi is not None:
                    nc.scalar.activation(hi[:, n], x[:, n], ACT.Copy,
                                         scale=column(G_COLS[m], n)).then_inc(act_hi_ready, 1)
                nc.scalar.activation(sq[:, parity], x[:, n], ACT.Square).then_inc(sq_ready, 1)

            def inverse_root(ps, scale, logs, ready, n):
                nc.scalar.activation(row_scale[:, :], ps, ACT.Ln, scale=scale, bias=eps[:, :]).then_inc(logs, 1)
                act.wait_ge(logs, n + 1)
                nc.scalar.activation(row_scale[:, :], row_scale[:, :], ACT.Exp, scale=-0.5).then_inc(ready, 1)

            def norm_scale(n):
                act.wait_ge(norm_wide, n + 1)
                inverse_root(aux_ps[2][:, :], 1.0 / D, norm_log, norm_ready, n)

            st = stages["E"]
            act.wait_ge(vec_ready, 2)
            def first_hi(slot):
                act.wait_ge(w_landed[slot], 16)
                nc.scalar.activation(w_hi[:, slot], w_raw[:, slot], ACT.Copy).then_inc(w_hi_ready, 1)

            for n in range(KT):
                tile_out(n, 0, n % 2, a_hi, xt_taken, n + 1)
                if n == 1:
                    first_hi(0)
            first_hi(1)
            first_hi(2)
            act.wait_ge(lb_diff, 1)
            nc.scalar.activation(lb_e, lb_d, ACT.Exp).then_inc(lb_exp, 1)

            def residual(stage, hi, m):
                def quad(i, last):
                    for j in range(4):
                        split_hi(act, stage, i, j)
                        if m is not None:
                            tile_out(i * 4 + j, m, j % 2, hi, block_taken, i * 4 + (stage.first + j + 1))

                run_quads(act, stage, quad)

            def conv_gates(i):
                for j in range(4):
                    split_hi(act, st, i, j)
                    if isinstance(i, int) and i == 0 and j == 0:
                        norm_scale(0)
                    if j % 2 == 0:
                        act.wait_ge(block_taken, i * 4 + (st.first + j + 1))
                        wait(act, gated, i * 2 + j // 2)
                        nc.scalar.activation(e_tanh, e_gate, ACT.Tanh, scale=0.5).then_inc(gate_tanh, 1)

            conv_gates(0)
            act.wait_ge(mem_in, 16)
            for m in range(MT):
                wait(act, mem_sq_ready, m)
                nc.scalar.activation(mem_sq, mem_tok[:, m], ACT.Square,
                                     accum_out=mem_ss[:, m:m + 1]).then_inc(mem_sq_ready, 1)
            conv_gates(1)
            act.wait_ge(mem_rstd, 1)
            for m in range(MT):
                nc.scalar.activation(mem_tok[:, m], mem_tok[:, m], ACT.Copy,
                                     scale=mem_rs[:, m:m + 1]).then_inc(mem_scaled, 1)
            def memory_hi(b):
                for n in (2 * b - 2, 2 * b - 1):
                    act.wait_ge(memt_ps, n + 1)
                    nc.scalar.activation(m_hi[:, n], aux_ps[n % 2][:, 0:N_MEM], ACT.Copy,
                                         scale=vec[:, V_MEM + n:V_MEM + n + 1]).then_inc(mem_hi, 1)
            act.wait_ge(pad_ready, 1)
            act.wait_ge(gated, CT)

            def conv_products(b):
                for m in range(BLOCK_PRODUCTS * b, min(BLOCK_PRODUCTS * (b + 1), CT * POOL_TAPS)):
                    c, n = divmod(m, POOL_TAPS)
                    adds = POOL_TAPS - 1
                    wait(act, conv_added, c * adds + max(1, n - 3) if n >= 3 else (c - 1) * adds + POOL_TAPS + n - 3)
                    k = DVE_TAPS + n
                    nc.scalar.activation(conv_pt[:, n % 3], u_pad[:, c, k:k + SEQ], ACT.Copy,
                                         scale=conv_w[:, CT * k + c:CT * k + c + 1]).then_inc(conv_product, 1)

            def gates(b):
                if b == 4:
                    act.wait_ge(block_taken, st.first + 12)
                    nc.scalar.activation(hg_k, hg_b, ACT.Tanh, scale=-0.5).then_inc(key_tanh, 1)
                    act.wait_ge(neg_abs, 1)
                    nc.scalar.activation(pre_1, pre_1, ACT.Exp).then_inc(scalar_step, 1)
                if b == 5:
                    act.wait_ge(lb_ready, 1)
                    act.wait_ge(scalar_step, 1)
                    nc.scalar.activation(pre_1, pre_1, ACT.Ln, bias=1.0).then_inc(log1p_a, 1)
                    nc.scalar.activation(ln_rest, lb_rest, ACT.Ln).then_inc(lb_logs, 1)
                    nc.scalar.activation(ln_scaled, lb_v, ACT.Ln, scale=2.0 ** 50).then_inc(lb_logs, 1)
                if b == 8:
                    act.wait_ge(log_pair, 1)
                    nc.scalar.activation(pre_2, pre_2, ACT.Exp).then_inc(scalar_step, 1)
                    act.wait_ge(scalar_step, 2)
                    nc.scalar.activation(pre_2, pre_2, ACT.Ln, bias=1.0).then_inc(log1p_b, 1)

            for b in range(16):
                if 1 <= b <= 4:
                    memory_hi(b)
                split_hi(act, st, 2 + b // 4, b % 4)
                conv_products(b)
                gates(b)

            def conv_squares():
                for c in range(CT):
                    act.wait_ge(centred, c + 1)
                    nc.scalar.activation(ln_sq[:, c], conv_y[:, c], ACT.Square).then_inc(cvar_sq, 1)

            def conv_scale():
                act.wait_ge(cvar_wide, 1)
                inverse_root(aux_ps[3][:, :], 1.0 / B_CH, cvar_log, cvar_ready, 0)

            def conv_tanh():
                for c in range(CT):
                    act.wait_ge(ln_out, c + 1)
                    nc.scalar.activation(ln_t[:, c], conv_y[:, c], ACT.Tanh).then_inc(ln_tanh, 1)

            def output_gate_tanh():
                act.wait_ge(block_taken, st.first + 24)
                nc.scalar.activation(gate_t, hg_g, ACT.Tanh, scale=0.5).then_inc(gate_tanh, 1)

            def conv_hi():
                for c in range(CT):
                    act.wait_ge(ln_act, c + 1)
                    nc.scalar.activation(a_hi[:, 4 + c], conv_y[:, c], ACT.Copy).then_inc(act_hi_ready, 1)

            def head_square(h):
                act.wait_ge(o_ps, h + 1)
                nc.scalar.activation(hg_sq, by_chunk(gemm_ps[3][:, :]), ACT.Square).then_inc(o_sq, 1)

            def head_hi(h):
                act.wait_ge(og_ready, h + 1)
                nc.scalar.activation(a_hi[:, h], hg_out, ACT.Copy).then_inc(act_hi_ready, 1)

            def head(h, first, second=False):
                def level(n):
                    act.wait_ge(e_arg, h * 8 + (n + 2))
                    halves = hg_e[:, (n + 1) % 4].rearrange("p (b s w) -> p s b w", s=2, w=LEVELS[n])
                    nc.scalar.activation(halves[:, 0], halves[:, 0], ACT.Exp, scale=-1.0)
                    nc.scalar.activation(halves[:, 1], halves[:, 1], ACT.Exp).then_inc(e_exp, 1)

                act.wait_ge(e_arg, h * 8 + 1)
                nc.scalar.activation(hg_e[:, 0], hg_e[:, 0], ACT.Exp).then_inc(e_exp, 1)
                level(0)
                if not first:
                    head_square(h - 1)
                act.wait_ge(vt_ps, h + 1)
                nc.scalar.activation(hg_v_tok, by_chunk(gemm_ps[1][:, :]), ACT.Copy).then_inc(vt_ready, 1)
                act.wait_ge(kdt_ps, h + 1)
                nc.scalar.activation(hg_kd_tok, by_chunk(gemm_ps[0][:, 0:3 * P]), ACT.Copy).then_inc(kdt_ready, 1)
                level(1)
                nc.scalar.activation(hg_qe, hg_b[:, h], ACT.Exp).then_inc(qe_exp, 1)
                if not first:
                    act.wait_ge(st_ready, h * 3)
                nc.scalar.activation(edge, hg_b[:, h, P - 1::P], ACT.Exp).then_inc(edge_ready, 1)
                level(2)
                if first:
                    conv_squares()
                level(3)
                if first:
                    output_gate_tanh()
                else:
                    head_hi(h - 1)
                level(4)
                if second:
                    conv_tanh()
                level(5)
                level(6)

            head(0, True)
            conv_scale()
            head(1, False, True)
            conv_hi()
            with act.Fori(2, A_HEADS) as h:
                head(h, False)
            head_square(A_HEADS - 1)
            head_hi(A_HEADS - 1)

            residual(stages["EO"], b_hi, 1)

            def memory_products(layer, n):
                st = stages[f"KV{layer}"]
                for at in range(8):
                    split_hi(act, st, at // 4, at % 4)
                    if at == 2:
                        norm_scale(n)
                for i in range(2, 4):
                    for j in range(4):
                        split_hi(act, st, i, j)
                        if j:
                            value_tile(layer, i, j - 1)
                    value_tile(layer, i, 3)

            def value_tile(layer, i, j):
                at = 4 * (i - 2) + j
                act.wait_ge(vf_turned, 8 * layer + at + 1)
                ps = by_chunk(aux_ps[j % 2][:, 0:MT * P])
                nc.scalar.activation(x_v[:, :, at * P:(at + 1) * P], ps, ACT.Copy).then_inc(vf_taken, 1)

            def cross_attention(layer):
                st = stages[f"XQ{layer}"]
                done = 4 * layer

                def softmax(h):
                    act.wait_ge(xs_max, done + h + 1)
                    wait(act, xpt_ps, done + h)
                    for t in range(TT):
                        mm = nc.scalar.activation(x_p[:, t], aux_ps[t // 2][:, (t % 2) * N_MEM:(t % 2 + 1) * N_MEM],
                                                  ACT.Exp, bias=xs_negmax[:, t:t + 1], accum_out=xs_sum[:, t:t + 1])
                    mm.then_inc(xs_exp, 1)

                def turned(h):
                    act.wait_ge(xpt_ps, done + h + 1)
                    wait(act, xo_ps, 2 * (done + h))
                    for m in range(MT):
                        mm = nc.scalar.activation(x_pt[:, m], aux_ps[2 + m][:, :], ACT.Copy)
                    mm.then_inc(xpt_ready, 1)

                def out_hi(h):
                    for d in range(2):
                        act.wait_ge(xo_ps, 2 * (done + h) + d + 1)
                        nc.scalar.activation(a_hi[:, 2 * h + d], aux_ps[2 + d][:, :], ACT.Copy).then_inc(act_hi_ready, 1)

                for h in range(X_HEADS + 2):
                    if h < X_HEADS:
                        split_hi(act, st, h // 2, 2 * (h % 2))
                    if h >= 2:
                        out_hi(h - 2)
                    if 1 <= h <= X_HEADS:
                        softmax(h - 1)
                    if h < X_HEADS:
                        split_hi(act, st, h // 2, 2 * (h % 2) + 1)
                    if 1 <= h <= X_HEADS:
                        turned(h - 1)

            def ffn(layer, n):
                for grp in range(3):
                    st = stages[f"FI{layer}{grp}"]
                    done = 22 * layer + 8 * grp

                    def quad(i, last):
                        for j in range(4):
                            split_hi(act, st, i, j)
                            if isinstance(i, int) and i == 0 and grp == 0 and j == 0:
                                norm_scale(n)
                            tile = i * 2 + (done + j // 2)
                            act.wait_ge(block_taken, i * 4 + (st.first + j + 1))
                            if j % 2 == 0:
                                wait(act, f_silu_ready, tile * 2 - 2)
                                nc.scalar.activation(f_tanh[:, j // 2], f_gate[:, j // 2], ACT.Tanh,
                                                     scale=0.5).then_inc(f_tanh_ready, 1)
                            else:
                                nc.scalar.activation(a_hi[:, i * 2 + j // 2], f_act[:, j // 2],
                                                     ACT.Copy).then_inc(act_hi_ready, 1)

                    if grp == 0:
                        quad(0, False)
                        with act.Fori(1, st.quads) as i:
                            quad(i, False)
                    else:
                        with act.Fori(0, st.quads) as i:
                            quad(i, False)
                    final = grp == 2
                    hi = b_hi if final and layer == 0 else None
                    residual(stages[f"FO{layer}{grp}"], hi, (3 if layer == 0 else 6) if final else None)

            def window_attention():
                st = stages["QKV"]
                for j in range(4):
                    split_hi(act, st, 0, j)
                    if j == 0:
                        norm_scale(3)
                for q in range(10):
                    n, m = q // 5, q % 5
                    rows = 64 if m == 4 else P
                    act.wait_ge(sv_ps, q + 1)
                    nc.scalar.activation(s_v[0:rows, n, m], aux_ps[q % 2][0:rows, 0:P], ACT.Copy).then_inc(sv_ready, 1)

                def softmax(w):
                    act.wait_ge(ss_max, w + 1)
                    wait(act, ss_norm, w - 1)
                    for b in range(2):
                        mm = nc.scalar.activation(s_e[:, w % 2, b], s_s[:, w % 2, b], ACT.Exp,
                                                  bias=ss_negmax[:, w % 2, b:b + 1], scale=C_HD ** -0.5,
                                                  accum_out=ss_sum[:, w % 2, b:b + 1])
                    mm.then_inc(ss_exp, 1)

                def turned(w):
                    act.wait_ge(spt_ps, w + 1)
                    wait(act, so_ps, w - 1)
                    src = gemm_ps[2][:, :].rearrange("p (b m q) -> p m b q", b=2, m=2)
                    dst = s_pt[:, w % 2].rearrange("p (b m q) -> p m b q", b=2, m=2)
                    nc.scalar.activation(dst[:, 0], src[:, 0], ACT.Copy)
                    nc.scalar.activation(dst[0:64, 1], src[0:64, 1], ACT.Copy).then_inc(spt_ready, 1)

                def out_hi(j):
                    act.wait_ge(so_ps, TT * (j + 1))
                    nc.scalar.activation(a_hi[:, j], gemm_ps[3][:, :], ACT.Copy).then_inc(act_hi_ready, 1)

                split_hi(act, st, 1, 0)
                split_hi(act, st, 1, 1)
                for w in range(TT * 8 + 3):
                    j = (w + 1) // TT + 1
                    if j < 8 and w % TT == TT - 1:
                        split_hi(act, st, 1 + j // 4, j % 4)
                    if w < TT * 8:
                        softmax(w)
                    if 2 <= w < TT * 8 + 2:
                        turned(w - 2)
                    if w >= 3 and (w - 3) % TT == TT - 1:
                        out_hi((w - 3) // TT)

            memory_products(0, 1)
            cross_attention(0)
            residual(stages["XO0"], b_hi, 2)
            ffn(0, 2)
            window_attention()
            residual(stages["SO"], b_hi, 4)
            memory_products(1, 4)
            cross_attention(1)
            residual(stages["XO1"], b_hi, 5)
            ffn(1, 5)
            act.wait_ge(fin_rstd, 1)
            for q in range(1, 2 * TT, 2):
                t = q // 2
                act.wait_ge(fin_ps, q + 1)
                nc.scalar.activation(o_tok[:, t, 512:1024], gemm_ps[q % 4][:, :], ACT.Copy,
                                     scale=rstd[:, t:t + 1]).then_inc(fin_odd, 1)

        @block.vector
        def _(dve):
            steps = [0]
            tt, ts, stt = nc.vector.tensor_tensor, nc.vector.tensor_scalar, nc.vector.scalar_tensor_tensor

            def step(ins):
                ins.then_inc(vector_step, 1)
                steps[0] += 1

            def settle(behind=0):
                wait(dve, vector_step, steps[0] - behind)

            dve.wait_ge(vec_turned, 1)
            nc.vector.tensor_copy(vec[:, :], aux_ps[0][:, 0:V_ROWS]).then_inc(vec_ready, 1)
            nc.vector.tensor_copy(conv_w[:, 0:B_KW * CT], aux_ps[0][:, P:P + B_KW * CT]).then_inc(vec_ready, 1)
            dve.wait_ge(vec_ready, 2)
            ts(onorm_half, vec[:, V_ONORM:V_ONORM + A_HEADS], 0.5 * P ** -0.5, None, ALU.mult)
            ts(lng_half, vec[:, V_LNG:V_LNG + CT], 0.5, None, ALU.mult)
            ts(lnb_half, vec[:, V_LNB:V_LNB + CT], 0.5, None, ALU.mult)
            tt(lb_d, vec[:, V_LB:V_LB + A_HEADS], vec[:, V_LB:V_LB + A_HEADS], ALU.subtract).then_inc(lb_diff, 1)

            def tile_lo(n, m, hi, lo, tiles):
                dve.wait_ge(act_hi_ready, n + (tiles + 1))
                stt(lo[:, n], x[:, n], column(G_COLS[m], n), hi[:, n].bitcast(F32), ALU.mult,
                    ALU.subtract).then_inc(act_lo_ready, 1)

            def first_lo(slot):
                dve.wait_ge(w_hi_ready, slot + 1)
                tt(w_lo[:, slot], w_raw[:, slot], w_hi[:, slot].bitcast(F32), ALU.subtract).then_inc(w_lo_ready, 1)

            for n in range(KT + 1):
                if n < KT:
                    dve.wait_ge(xt_done, n + 1)
                    nc.vector.tensor_copy(x[:, n], aux_ps[(n + 1) % 4][:, :]).then_inc(xt_taken, 1)
                if n:
                    tile_lo(n - 1, 0, a_hi, a_lo, TILES["x0"])
                if n == 2:
                    first_lo(0)
            first_lo(1)
            first_lo(2)
            dve.wait_ge(consts_in, 16 * 4)
            ts(sink8, sink8, C_HD ** 0.5, None, ALU.mult)

            dve.wait_ge(lb_exp, 1)
            step(nc.vector.reciprocal(lb_r, lb_e))
            settle()
            step(tt(lb_r, lb_e, lb_r, ALU.mult))
            settle()
            step(tt(lb_v, lb_r, lb_r, ALU.subtract))
            settle()
            step(ts(lb_v, lb_v, LB_FLOOR, 1.0 - 1e-6, ALU.max, ALU.min))
            settle()
            step(ts(lb_rest, lb_v, -1.0, 1.0, ALU.mult, ALU.add))
            settle()
            ts(lb_half, lb_rest, 0.5, None, ALU.mult).then_inc(lb_ready, 1)

            def mean_squares(dst, ps, scale, ready):
                ts(dst, ps, scale, EPS, ALU.mult, ALU.add).then_inc(ready, 1)

            def scaled(dst, stage, i, j, factor=None, banks=4):
                dve.wait_ge(block_done, i * 4 + (stage.first + j + 1))
                if factor is None:
                    ins = tt(dst, gemm_ps[j % banks][:, :], row_scale[:, :], ALU.mult)
                else:
                    ins = stt(dst, gemm_ps[j % banks][:, :], factor, row_scale[:, :], ALU.mult, ALU.mult)
                ins.then_inc(block_taken, 1)
                return i * 4 + (stage.first + j + 1)

            st = stages["E"]
            dve.wait_ge(norm_ready, 1)
            for i in range(2):
                if i:
                    dve.wait_ge(mem_sq_ready, MT)
                    mean_squares(mem_m, mem_ss, 1.0 / D, mem_ms)
                for j in range(4):
                    c = 2 * i + j // 2
                    wait(dve, gated, c)
                    taken = scaled(e_half if j % 2 else e_gate, st, i, j, 0.5 if j % 2 else None)
                    split_lo(dve, st, i, j)
                    if j % 2:
                        dve.wait_ge(gate_tanh, c + 1)
                        dve.wait_ge(block_taken, taken)
                        stt(u_pad[:, c, PAD:], e_tanh, 1.0, e_half, ALU.add, ALU.mult).then_inc(gated, 1)
            def memory_lo(b):
                for n in (2 * b - 2, 2 * b - 1):
                    dve.wait_ge(mem_hi, n + 1)
                    stt(m_lo[:, n], aux_ps[n % 2][:, 0:N_MEM], vec[:, V_MEM + n:V_MEM + n + 1],
                        m_hi[:, n].bitcast(F32), ALU.mult, ALU.subtract).then_inc(mem_lo, 1)

            dve.wait_ge(pad_ready, 1)
            dve.wait_ge(gated, CT)

            def tap(c, k):
                return u_pad[:, c, k:k + SEQ], conv_w[:, CT * k:CT * k + CT].rearrange("p (c o) -> p c o", o=1)[:, c]

            def conv_taps(b):
                for s in range(sum(BLOCK_TAPS[:b]), sum(BLOCK_TAPS[:b + 1])):
                    c, k = divmod(s, DVE_TAPS)
                    u, w = tap(c, k)
                    into = conv_b2 if k % 2 else conv_y[:, c]
                    if k >= 2:
                        settle(1)
                    if k == 0:
                        step(ts(into, u, w, column(V_CONVB, c), ALU.mult, ALU.add))
                    elif k == 1:
                        settle(1)
                        step(ts(into, u, w, None, ALU.mult))
                    else:
                        step(stt(into, u, w, into, ALU.mult, ALU.add))
                    if k == DVE_TAPS - 1:
                        conv_merge(c)

            def conv_merge(c):
                y = conv_y[:, c]
                settle()
                step(tt(y, y, conv_b2, ALU.add))
                settle()
                dve.wait_ge(conv_added, c * (POOL_TAPS - 1) + (POOL_TAPS - 1))
                tt(y, y, conv_p[:, c % 2], ALU.add).then_inc(conv_merged, 1)

            def gates(b):
                if b == 4:
                    stt(pre_1, hg_b, -1.0, hg_b, ALU.mult, ALU.min).then_inc(neg_abs, 1)
                    dve.wait_ge(key_tanh, 1)
                    for h in range(A_HEADS):
                        step(ts(hg_k[:, h], hg_k[:, h], lb_half[:, h:h + 1], lb_half[:, h:h + 1], ALU.mult, ALU.add))
                if b == 5:
                    dve.wait_ge(log1p_a, 1)
                    step(stt(pre_1, hg_b, 0.0, pre_1, ALU.min, ALU.subtract))
                    dve.wait_ge(lb_logs, 2)
                    step(ts(ln_lb, ln_scaled, -LN2_50, None, ALU.add))
                if b == 6:
                    settle()
                    for h in range(A_HEADS):
                        step(ts(hg_b[:, h], pre_1[:, h], ln_rest[:, h:h + 1], ln_lb[:, h:h + 1], ALU.add, ALU.max))
                        step(ts(pre_2[:, h], pre_1[:, h], ln_rest[:, h:h + 1], ln_lb[:, h:h + 1], ALU.add, ALU.min))
                    settle()
                    tt(pre_2, pre_2, hg_b, ALU.subtract).then_inc(log_pair, 1)
                if b == 10:
                    dve.wait_ge(log1p_b, 1)
                    step(tt(pre_2, pre_2, hg_b, ALU.add))
                    settle()
                    for h in range(A_HEADS):
                        ins = nc.vector.tensor_tensor_scan(hg_b[:, h], scan_mask, pre_2[:, h], 0.0, ALU.mult, ALU.add)
                    ins.then_inc(gates_ready, 1)
                    dve.wait_ge(gates_ready, 1)

            for b in range(16):
                if 1 <= b <= 4:
                    memory_lo(b)
                scaled(early[:, (1, 0, 2, 3)[b // 4], b % 4], st, 2 + b // 4, b % 4)
                split_lo(dve, st, 2 + b // 4, b % 4)
                conv_taps(b)
                gates(b)
            dve.wait_ge(conv_merged, CT)

            def conv_centre():
                dve.wait_ge(mean_wide, 1)
                for c in range(CT):
                    stt(conv_y[:, c], aux_ps[2][:, :], -1.0 / B_CH, conv_y[:, c], ALU.mult,
                        ALU.add).then_inc(centred, 1)

            def conv_norm():
                dve.wait_ge(cvar_ready, 1)
                dve.wait_ge(centred, CT)
                for c in range(CT):
                    step(tt(conv_y[:, c], conv_y[:, c], row_scale[:, :], ALU.mult))
                for c in range(CT):
                    settle(CT - 1 - c)
                    ts(conv_y[:, c], conv_y[:, c], lng_half[:, c:c + 1], lnb_half[:, c:c + 1], ALU.mult,
                       ALU.add).then_inc(ln_out, 1)

            def conv_silu():
                for c in range(CT):
                    dve.wait_ge(ln_tanh, c + 1)
                    stt(conv_y[:, c], ln_t[:, c], 1.0, conv_y[:, c], ALU.add, ALU.mult).then_inc(ln_act, 1)

            def gate_silu():
                dve.wait_ge(gate_tanh, 5)
                stt(hg_g, gate_t, 1.0, hg_g, ALU.add, ALU.mult).then_inc(gated, 1)

            def conv_lo():
                for c in range(CT):
                    dve.wait_ge(act_hi_ready, TILES["mix0"] + c + 2)
                    tt(a_lo[:, 4 + c], conv_y[:, c], a_hi[:, 4 + c].bitcast(F32), ALU.subtract).then_inc(act_lo_ready, 1)

            def bcast(ap, n):
                return ap.to_broadcast([P, TT, n])

            def head_mean_squares(h):
                dve.wait_ge(o_sq, h + 1)
                step(nc.vector.tensor_reduce(o_m, hg_sq, AX_X, ALU.add))
                settle()
                mean_squares(o_m, o_m, 1.0 / (P * P), o_ms)

            def head_norm(h):
                dve.wait_ge(o_rstd, h + 1)
                tt(hg_on, by_chunk(gemm_ps[3][:, :]), bcast(o_r.unsqueeze(2), P), ALU.mult).then_inc(on_ready, 1)

            def head_gate(h):
                dve.wait_ge(ont_ps, h + 1)
                dve.wait_ge(gated, CT + 1)
                stt(hg_out, aux_ps[2][:, :], onorm_half[:, h:h + 1], hg_g[:, h], ALU.mult,
                    ALU.mult).then_inc(og_ready, 1)

            def head_lo(h):
                dve.wait_ge(act_hi_ready, TILES["mix0"] + (CT if h else 0) + h + 1)
                tt(a_lo[:, h], hg_out, a_hi[:, h].bitcast(F32), ALU.subtract).then_inc(act_lo_ready, 1)

            for h in range(A_HEADS):
                def level_product(n):
                    dve.wait_ge(e_exp, h * 8 + (n + 2))
                    wait(dve, lev_ps, h * 8 + n)
                    size = LEVELS[n]
                    e = hg_e[:, (n + 1) % 4].rearrange("p (b s w) -> p s b w", s=2, w=size)
                    qk = hg_qk[:, n % 2].rearrange("p (b s w) -> p s b w", s=2, w=size)
                    for s_, src in ((0, hg_k), (1, hg_q)):
                        v = src[:, h].rearrange("p (b s w) -> p s b w", s=2, w=size)[:, s_]
                        ins = tt(qk[:, s_], e[:, s_], v, ALU.mult)
                    ins.then_inc(lev_ready, 1)

                def level_take(n):
                    dve.wait_ge(lev_ps, h * 8 + (n + 2))
                    if n < 0:
                        wait(dve, o_ps, h)
                        tt(hg_scores, by_chunk(aux_ps[0][:, :]), ident[:, :].unsqueeze(1).to_broadcast([P, TT, P]),
                           ALU.mult).then_inc(lev_taken, 1)
                    else:
                        dve.wait_ge(lev_taken, h * 8 + (n + 1))
                        mask = lev_mask[:, n].bitcast(U32).unsqueeze(1).to_broadcast([P, TT, P])
                        nc.vector.copy_predicated(hg_scores, mask, by_chunk(aux_ps[(n + 1) % 2][:, :])).then_inc(lev_taken, 1)

                dve.wait_ge(e_exp, h * 8 + 1)
                tt(hg_e[:, 0], hg_e[:, 0], hg_k[:, h], ALU.mult).then_inc(kd_ready, 1)
                level_product(0)
                if h:
                    head_mean_squares(h - 1)
                level_take(-1)
                level_product(1)
                level_take(0)
                if h == 0:
                    conv_centre()
                dve.wait_ge(qe_exp, h + 1)
                tt(hg_qe, hg_qe, hg_q[:, h], ALU.mult).then_inc(qe_ready, 1)
                dve.wait_ge(st_ps, h + 1)
                dve.wait_ge(edge_ready, h + 1)
                for c in range(3):
                    ps = gemm_ps[2][:, c * P:(c + 1) * P]
                    if c == 0:
                        nc.vector.tensor_copy(hg_state[:, 0], ps).then_inc(st_ready, 1)
                    else:
                        dve.wait_ge(st_ready, h * 3 + c)
                        stt(hg_state[:, c], hg_state[:, c - 1], edge[:, c:c + 1], ps, ALU.mult,
                            ALU.add).then_inc(st_ready, 1)
                for n in range(2, len(LEVELS)):
                    if h and n == 2:
                        head_norm(h - 1)
                    level_product(n)
                    level_take(n - 1)
                    if h and n == 2:
                        head_gate(h - 1)
                    if h == 2 and n == 3:
                        conv_lo()
                    if h and n == 3:
                        head_lo(h - 1)
                    if h == 1 and n == 3:
                        conv_norm()
                    if h == 1 and n == 6:
                        conv_silu()
                level_take(len(LEVELS) - 1)
                if h == 0:
                    gate_silu()
            head_mean_squares(A_HEADS - 1)
            head_norm(A_HEADS - 1)
            head_gate(A_HEADS - 1)
            head_lo(A_HEADS - 1)

            def residual(stage, hi, lo, m, tiles, bias=None):
                def quad(i, last):
                    for j in range(4):
                        n = i * 4 + j
                        dve.wait_ge(block_done, i * 4 + (stage.first + j + 1))
                        if bias is None:
                            ins = tt(x[:, n], gemm_ps[j][:, :], x[:, n], ALU.add)
                        else:
                            ins = stt(x[:, n], gemm_ps[j][:, :], column(bias, n), x[:, n], ALU.add, ALU.add)
                        ins.then_inc(block_taken, 1)
                        split_lo(dve, stage, i, j)
                        if hi is not None:
                            tile_lo(n, m, hi, lo, tiles)

                run_quads(dve, stage, quad)

            residual(stages["EO"], b_hi, b_lo, 1, TILES["x1"])

            def memory_products(layer, n):
                st = stages[f"KV{layer}"]
                for i in range(4):
                    for j in range(4):
                        dve.wait_ge(block_done, st.first + 4 * i + j + 1)
                        if i < 2:
                            dst = x_k[:, 4 * i + j]
                        else:
                            wait(dve, vf_turned, 8 * layer + 4 * (i - 2) + j - 1)
                            dst = v_feat[:, j % 2]
                        nc.vector.tensor_copy(dst, gemm_ps[j][:, 0:N_MEM]).then_inc(block_taken, 1)
                        split_lo(dve, st, i, j)
                dve.wait_ge(norm_ready, n + 1)

            def cross_attention(layer):
                st = stages[f"XQ{layer}"]
                done = 4 * layer
                tiles = TILES[f"att{layer}"]

                def query(h, d):
                    if d == 0:
                        wait(dve, xs_ps, done + h - 1)
                    scaled(x_q[:, h % 2, d], st, h // 2, 2 * (h % 2) + d, X_HD ** -0.5)
                    split_lo(dve, st, h // 2, 2 * (h % 2) + d)

                def out_lo(h):
                    for d in range(2):
                        dve.wait_ge(act_hi_ready, tiles + 2 * h + d + 1)
                        tt(a_lo[:, 2 * h + d], aux_ps[2 + d][:, :], a_hi[:, 2 * h + d].bitcast(F32),
                           ALU.subtract).then_inc(act_lo_ready, 1)

                def maxima(h):
                    dve.wait_ge(xs_ps, done + h + 1)
                    for b in range(2):
                        ps = aux_ps[b][:, :].rearrange("p (t m) -> p t m", m=N_MEM)
                        ins = nc.vector.tensor_reduce(xs_negmax[:, 2 * b:2 * b + 2], ps, AX_X, ALU.max, negate=True)
                    ins.then_inc(xs_max, 1)

                def normalise(h):
                    dve.wait_ge(xs_exp, done + h + 1)
                    step(nc.vector.reciprocal(xs_rec, xs_sum))
                    settle()
                    for t in range(TT):
                        ins = ts(x_p[:, t], x_p[:, t], xs_rec[:, t:t + 1], None, ALU.mult)
                    ins.then_inc(xs_norm, 1)

                for h in range(X_HEADS + 2):
                    if h < X_HEADS:
                        query(h, 0)
                    if h >= 2:
                        out_lo(h - 2)
                    if 1 <= h <= X_HEADS:
                        maxima(h - 1)
                        normalise(h - 1)
                    if h < X_HEADS:
                        query(h, 1)

            def ffn(layer, n):
                for grp, size in enumerate(FF_GROUPS):
                    st = stages[f"FI{layer}{grp}"]
                    done = 22 * layer + 8 * grp
                    tiles = TILES[f"h{layer}{grp}"]

                    def quad(i):
                        for j in range(4):
                            s2 = j // 2
                            tile = i * 2 + (done + s2)
                            if j % 2 == 0:
                                wait(dve, f_silu_ready, tile * 2 - 2)
                                taken = scaled(f_gate[:, s2], st, i, j)
                                split_lo(dve, st, i, j)
                                dve.wait_ge(f_tanh_ready, tile + 1)
                                dve.wait_ge(block_taken, taken)
                                stt(f_silu[:, s2], f_tanh[:, s2], 1.0, f_gate[:, s2], ALU.add,
                                    ALU.mult).then_inc(f_silu_ready, 1)
                                dve.wait_ge(f_silu_ready, tile * 2 + 1)
                                stt(f_silu[:, s2], f_silu[:, s2], 0.5, row_scale[:, :], ALU.mult,
                                    ALU.mult).then_inc(f_silu_ready, 1)
                            else:
                                dve.wait_ge(block_done, i * 4 + (st.first + j + 1))
                                dve.wait_ge(f_silu_ready, tile * 2 + 2)
                                tt(f_act[:, s2], gemm_ps[j][:, :], f_silu[:, s2], ALU.mult).then_inc(block_taken, 1)
                                split_lo(dve, st, i, j)
                                dve.wait_ge(act_hi_ready, i * 2 + (tiles + s2 + 1))
                                tt(a_lo[:, i * 2 + s2], f_act[:, s2], a_hi[:, i * 2 + s2].bitcast(F32),
                                   ALU.subtract).then_inc(act_lo_ready, 1)

                    if grp == 0:
                        dve.wait_ge(norm_ready, n + 1)
                        quad(0)
                    with dve.Fori(1 if grp == 0 else 0, st.quads) as i:
                        quad(i)
                    so = stages[f"FO{layer}{grp}"]
                    if grp == 2 and layer == 0:
                        residual(so, b_hi, b_lo, 3, TILES["x3"])
                    else:
                        residual(so, None, None, None, None)

            def window_attention():
                st = stages["QKV"]
                dve.wait_ge(norm_ready, 4)
                for j in range(4):
                    dst = (s_k if j < 2 else s_vf)[:, j % 2, 64:]
                    taken = scaled(dst, st, 0, j)
                    dve.wait_ge(block_taken, taken)
                    ins = ts(dst, dst, vec[:, V_BKV + j:V_BKV + j + 1], None, ALU.add)
                    if j == 3:
                        ins.then_inc(sv_pad, 1)
                    split_lo(dve, st, 0, j)

                def query(j):
                    wait(dve, ss_ps, TT * (j - 1))
                    dst = s_q[:, j % 2]
                    taken = scaled(dst, st, 1 + j // 4, j % 4, banks=2)
                    dve.wait_ge(block_taken, taken)
                    ts(dst, dst, vec[:, V_BQ + j:V_BQ + j + 1], None, ALU.add).then_inc(sq_biased, 1)

                def scores(w):
                    j, t = w // TT, w % TT
                    dve.wait_ge(ss_ps, w + 1)
                    wait(dve, ss_exp, w - 1)
                    for b in range(2):
                        head = 8 * (j // 4) + j % 4 + 4 * b
                        stt(s_s[:, w % 2, b, 0:WIN], s_dist[:, 0 if t == 0 else 1], s_slope[:, head:head + 1],
                            aux_ps[2 * (w % 2) + b][:, 0:WIN], ALU.mult, ALU.add)
                    head = 8 * (j // 4) + j % 4
                    nc.vector.tensor_copy(s_s[:, w % 2, :, WIN], sink8[:, head:head + 5:4]).then_inc(ss_ready, 1)
                    dve.wait_ge(ss_ready, w + 1)
                    step(nc.vector.tensor_reduce(ss_negmax[:, w % 2], s_s[:, w % 2], AX_X, ALU.max))
                    settle()
                    ts(ss_negmax[:, w % 2], ss_negmax[:, w % 2], -C_HD ** -0.5, None, ALU.mult).then_inc(ss_max, 1)

                def normalise(w):
                    dve.wait_ge(ss_exp, w + 1)
                    step(nc.vector.reciprocal(ss_rec[:, w % 2], ss_sum[:, w % 2]))
                    settle()
                    wait(dve, spt_ps, w - 1)
                    for b in range(2):
                        ins = ts(s_p[:, w % 2, b], s_e[:, w % 2, b, 0:WIN], ss_rec[:, w % 2, b:b + 1], None, ALU.mult)
                    ins.then_inc(ss_norm, 1)

                def out_lo(j):
                    dve.wait_ge(act_hi_ready, TILES["mix1"] + j + 1)
                    tt(a_lo[:, j], gemm_ps[3][:, :], a_hi[:, j].bitcast(F32), ALU.subtract).then_inc(act_lo_ready, 1)

                split_lo(dve, st, 1, 0)
                query(0)
                split_lo(dve, st, 1, 1)
                for w in range(TT * 8 + 3):
                    j = w // TT + 1
                    if j < 8 and w % TT == TT - 1:
                        query(j)
                    if w >= TT + 3 and w % TT == TT - 1:
                        out_lo((w - 4) // TT)
                    if w < TT * 8:
                        scores(w)
                    if 1 <= w <= TT * 8:
                        normalise(w - 1)
                    if j < 7 and w % TT == TT - 1:
                        split_lo(dve, st, 1 + (j + 1) // 4, (j + 1) % 4)
                out_lo(7)

            memory_products(0, 1)
            cross_attention(0)
            residual(stages["XO0"], b_hi, b_lo, 2, TILES["x2"])
            ffn(0, 2)
            window_attention()
            residual(stages["SO"], b_hi, b_lo, 4, TILES["x4"], V_BO)
            memory_products(1, 4)
            cross_attention(1)
            residual(stages["XO1"], b_hi, b_lo, 5, TILES["x5"])
            ffn(1, 5)
            for n in range(KT):
                dve.wait_ge(sq_ready, 48 + n + 1)
                ts(x[:, n], x[:, n], vec[:, V_FINAL + n:V_FINAL + n + 1], None, ALU.mult).then_inc(fin_scaled, 1)
            dve.wait_ge(fin_sums, 1)
            mean_squares(ms, aux_ps[3][:, 0:TT], 1.0 / D, fin_ms)
            dve.wait_ge(fin_rstd, 1)
            for q in range(0, 2 * TT, 2):
                dve.wait_ge(fin_ps, q + 1)
                ts(o_tok[:, q // 2, 0:512], gemm_ps[q % 4][:, :], rstd[:, q // 2:q // 2 + 1], None,
                   ALU.mult).then_inc(fin_even, 1)

        @block.gpsimd
        def _(pool):
            def power(dst, src, n, ready):
                nc.gpsimd.tensor_tensor(dst, src, minus_half[:, 0:n], ALU.pow).then_inc(ready, 1)

            def clear_sums(n):
                nc.gpsimd.memset(sumsq[:, :], 0.0).then_inc(sumsq_clear, 1)
                pool.wait_ge(sumsq_clear, n + 1)

            nc.gpsimd.memset(ones[:, :], 1.0).then_inc(fills_ready, 1)
            nc.gpsimd.memset(minus_half[:, :], -0.5).then_inc(fills_ready, 1)
            nc.gpsimd.memset(eps[:, :], EPS).then_inc(fills_ready, 1)
            pool.wait_ge(fills_ready, 3)

            def add_squares(m, n, parity):
                pool.wait_ge(sq_ready, n + (8 * m + 1))
                wait(pool, sumsq_added, n + 8 * m)
                nc.gpsimd.tensor_tensor(sumsq[:, :], sumsq[:, :], sq[:, parity], ALU.add).then_inc(sumsq_added, 1)

            def norm(m):
                if m:
                    pool.wait_ge(norm_wide, m)
                clear_sums(m)
                with pool.Fori(0, KT // 2) as i:
                    for j in range(2):
                        add_squares(m, i * 2 + j, j)

            norm(0)
            pool.wait_ge(xt_done, KT)
            nc.gpsimd.memset(u_pad[:, :, 0:PAD], 0.0).then_inc(pad_ready, 1)
            pool.wait_ge(mem_ms, 1)
            power(mem_rs, mem_m, MT, mem_rstd)
            for c in range(CT):
                wait(pool, conv_merged, c - 1)
                total = conv_p[:, c % 2]
                for n in range(1, POOL_TAPS):
                    pool.wait_ge(conv_product, c * POOL_TAPS + n + 1)
                    wait(pool, conv_added, c * (POOL_TAPS - 1) + n - 1)
                    nc.gpsimd.tensor_tensor(total, conv_pt[:, 0] if n == 1 else total, conv_pt[:, n % 3],
                                            ALU.add).then_inc(conv_added, 1)
            pool.wait_ge(gates_ready, 1)
            pool.wait_ge(conv_merged, CT)
            for h in range(A_HEADS):
                wait(pool, lev_ready, h * 7 - 3)
                b3 = by_chunk(hg_b[:, h])
                nc.gpsimd.tensor_tensor(by_chunk(hg_e[:, 0]), b3[:, :, P - 1:P].to_broadcast([P, TT, P]), b3,
                                        ALU.subtract).then_inc(e_arg, 1)
                for n, size in enumerate(LEVELS):
                    if n < 3:
                        wait(pool, lev_ready, h * 7 + n - 2)
                    elif n == 3:
                        pool.wait_ge(kdt_ps, h + 1)
                    else:
                        pool.wait_ge(lev_ready, h * 7 + n - 3)
                    b = hg_b[:, h].rearrange("p (b w) -> p b w", w=2 * size)
                    e = hg_e[:, (n + 1) % 4].rearrange("p (b w) -> p b w", w=2 * size)
                    mid = b[:, :, size - 1:size].to_broadcast([P, SEQ // (2 * size), 2 * size])
                    nc.gpsimd.tensor_tensor(e, b, mid, ALU.subtract).then_inc(e_arg, 1)
                    if h and n == 2:
                        pool.wait_ge(o_ms, h)
                        power(o_r, o_m, TT, o_rstd)
            pool.wait_ge(o_ms, A_HEADS)
            power(o_r, o_m, TT, o_rstd)
            norm(1)
            norm(2)
            norm(3)
            pool.wait_ge(block_done, stages["QKV"].first)
            nc.gpsimd.memset(s_k[:, :, 0:64], 0.0)
            nc.gpsimd.memset(s_vf[:, :, 0:64], 0.0).then_inc(sv_pad, 1)
            for m in range(4, 7):
                norm(m)
            pool.wait_ge(fin_ms, 1)
            power(rstd, ms, TT, fin_rstd)


IN = ["x", "mem", "norm_mix", "norm_xattn", "norm_ffn", "norm_mem", "norm_final", "even_w_in", "even_w_out",
      "hgrn_lb_logits", "hgrn_out_norm", "conv_w", "conv_b", "conv_ln_g", "conv_ln_b", "swa_w_qkv", "swa_b_qkv",
      "swa_sinks", "swa_w_o", "swa_b_o", "xattn_w_q", "xattn_w_kv", "xattn_w_o", "ffn_w_in", "ffn_w_out"]


def shape_constants():
    ident = np.eye(P, dtype=np.float32)
    scan = np.ones(SEQ, np.float32)
    scan[::P] = 0
    s, t = np.arange(P)[:, None], np.arange(P)[None, :]
    masks = [((s // (2 * w) == t // (2 * w)) & (s % (2 * w) < w) & (t % (2 * w) >= w)) for w in LEVELS]
    hgrn = np.concatenate([np.broadcast_to(scan, (P, SEQ))] + [m.astype(np.float32) for m in masks], axis=1)
    r, c = np.arange(P)[:, None], np.arange(WIN)[None, :]
    inside = np.where(r < CHUNK, c < 2 * CHUNK, c >= CHUNK)
    first = inside & (c >= CHUNK)
    dist = np.stack([np.where(m, -np.abs(r + CHUNK - c).astype(np.float32), np.float32(-1e33)) for m in (first, inside)], 1)
    slope = np.broadcast_to((2.0 ** (-8.0 * np.arange(1, C_QH + 1) / C_QH) * C_HD ** 0.5).astype(np.float32), (P, C_QH))
    return {"ident": ident, "hgrn": np.ascontiguousarray(hgrn, np.float32),
            "dist": np.ascontiguousarray(dist, np.float32), "slope": np.ascontiguousarray(slope)}


def kernel(**inputs):
    import concourse.bacc as bacc
    from concourse.bass_utils import run_bass_kernel_spmd

    nc = bacc.Bacc("TRN2", target_bir_lowering=False, num_devices=1)
    arrays, aps = {}, {}
    for name in IN:
        v = np.ascontiguousarray(inputs[name])
        arrays["in_" + name] = v
        aps[name] = nc.dram_tensor("in_" + name, v.shape, mybir.dt.from_np(v.dtype), kind="ExternalInput").ap()
    consts = {}
    for name, v in shape_constants().items():
        arrays["const_" + name] = v
        consts[name] = nc.dram_tensor("const_" + name, v.shape, F32, kind="ExternalInput").ap()
    out = nc.dram_tensor("out", (1, SEQ, D), F32, kind="ExternalOutput").ap()
    trunk_kernel(nc, aps, consts, out)
    r = run_bass_kernel_spmd(nc, [arrays], core_ids=[0])
    return r.results[0]["out"]
```
